# Optimizing a Trainium2 kernel written in Bass

```python
import math
import jax, jax.numpy as jnp
from jax import lax
import numpy as np

D_MODEL = 1024
BATCH = 1
SEQ = 256
DEPTH = 2

HEAD_DIM = 64
N_HEADS = D_MODEL // HEAD_DIM
D_FF = 4 * D_MODEL
N_MIXERS = 2
MOBA_BLOCK = 256
MOBA_TOPK = 3
MOBA_Q_CHUNK = 8
SB_Q_BLOCK = 128
REL_BUCKETS = 32
REL_MAX_DIST = 128
LN_EPS = 1e-5
DEEPNORM_ALPHA = (2.0 * DEPTH) ** 0.25
DEEPNORM_BETA = (8.0 * DEPTH) ** -0.25

kernel_name = "moba_stickbreaking_deepnorm_hybrid"

def layer_norm(x, g, b):
    xf = x.astype(jnp.float32)
    mu = jnp.mean(xf, axis=-1, keepdims=True)
    var = jnp.mean(jnp.square(xf - mu), axis=-1, keepdims=True)
    y = (xf - mu) * lax.rsqrt(var + LN_EPS)
    return (y * g.astype(jnp.float32) + b.astype(jnp.float32)).astype(x.dtype)

def t5_bucket(dist):
    n = jnp.maximum(dist, 0)
    max_exact = REL_BUCKETS // 2
    nf = jnp.maximum(n, 1).astype(jnp.float32)
    large = max_exact + (jnp.log(nf / max_exact) / math.log(REL_MAX_DIST / max_exact)
                         * (REL_BUCKETS - max_exact)).astype(jnp.int32)
    large = jnp.minimum(large, REL_BUCKETS - 1)
    return jnp.where(n < max_exact, n, large)

def moba_attention(q, k, v, rel_bias):
    B, H, S, dh = q.shape
    nb = -(-S // MOBA_BLOCK)
    s_pad = nb * MOBA_BLOCK
    topk = min(MOBA_TOPK, nb)
    pad = ((0, 0), (0, 0), (0, s_pad - S), (0, 0))
    k_pad = jnp.pad(k, pad)
    v_pad = jnp.pad(v, pad)
    k_blk = k_pad.reshape(B, H, nb, MOBA_BLOCK, dh)
    v_blk = v_pad.reshape(B, H, nb, MOBA_BLOCK, dh)
    k_mean = jnp.mean(k_blk.astype(jnp.float32), axis=3)

    q_blk_id = jnp.arange(S) // MOBA_BLOCK
    gate = jnp.einsum('bhsd,bhnd->bhsn', q.astype(jnp.float32), k_mean)
    past = jnp.arange(nb)[None, :] < q_blk_id[:, None]
    gate = jnp.where(past, gate, -jnp.inf)
    _, sel = lax.top_k(gate, topk)
    sel_valid = sel < q_blk_id[:, None]

    nc = S // MOBA_Q_CHUNK

    def to_chunks(a):
        a = a.reshape((B, H, nc, MOBA_Q_CHUNK) + a.shape[3:])
        return jnp.moveaxis(a, 2, 0)

    table_t = rel_bias.T.astype(jnp.float32)
    head_ix = jnp.arange(H)[None, :, None, None, None]
    gather_blocks = jax.vmap(jax.vmap(lambda blk, ix: blk[ix]))
    scale = dh ** -0.5
    w_ar = jnp.arange(MOBA_BLOCK)

    def chunk_fn(args):
        qc, selc, validc, c = args
        t = c * MOBA_Q_CHUNK + jnp.arange(MOBA_Q_CHUNK)
        kg = gather_blocks(k_blk, selc)
        vg = gather_blocks(v_blk, selc)
        key_pos_g = selc[..., None] * MOBA_BLOCK + w_ar
        bias_g = table_t[head_ix, t5_bucket(t[:, None, None] - key_pos_g)]
        s_g = jnp.einsum('bhqd,bhqkwd->bhqkw', qc, kg).astype(jnp.float32) * scale + bias_g
        s_g = jnp.where(validc[..., None], s_g, -jnp.inf)
        start = ((c * MOBA_Q_CHUNK) // MOBA_BLOCK) * MOBA_BLOCK
        ko = lax.dynamic_slice_in_dim(k_pad, start, MOBA_BLOCK, axis=2)
        vo = lax.dynamic_slice_in_dim(v_pad, start, MOBA_BLOCK, axis=2)
        rel_o = t[:, None] - (start + w_ar)[None, :]
        bias_o = table_t[:, t5_bucket(rel_o)]
        s_o = jnp.einsum('bhqd,bhwd->bhqw', qc, ko).astype(jnp.float32) * scale + bias_o
        s_o = jnp.where(rel_o >= 0, s_o, -jnp.inf)
        logits = jnp.concatenate(
            [s_g.reshape(B, H, MOBA_Q_CHUNK, topk * MOBA_BLOCK), s_o], axis=-1)
        p = jax.nn.softmax(logits, axis=-1).astype(v.dtype)
        p_g = p[..., :topk * MOBA_BLOCK].reshape(B, H, MOBA_Q_CHUNK, topk, MOBA_BLOCK)
        p_o = p[..., topk * MOBA_BLOCK:]
        return (jnp.einsum('bhqkw,bhqkwd->bhqd', p_g, vg)
                + jnp.einsum('bhqw,bhwd->bhqd', p_o, vo))

    out = lax.map(chunk_fn, (to_chunks(q), to_chunks(sel), to_chunks(sel_valid),
                             jnp.arange(nc)))
    return jnp.moveaxis(out, 0, 2).reshape(B, H, S, dh)

def stick_breaking_attention(q, k, v):
    B, H, S, dh = q.shape
    scale = dh ** -0.5
    outs = []
    for t0 in range(0, S, SB_Q_BLOCK):
        end = t0 + SB_Q_BLOCK
        qb = q[:, :, t0:end]
        kk = k[:, :, :end]
        vv = v[:, :, :end]
        z = jnp.einsum('bhqd,bhsd->bhqs', qb, kk).astype(jnp.float32) * scale
        t = t0 + jnp.arange(SB_Q_BLOCK)[:, None]
        s = jnp.arange(end)[None, :]
        causal = s < t
        log_keep = jnp.where(causal, jax.nn.log_sigmoid(-z), 0.0)
        after = lax.cumsum(log_keep, axis=3, reverse=True) - log_keep
        a = jnp.where(causal, jnp.exp(jax.nn.log_sigmoid(z) + after), 0.0)
        outs.append(jnp.einsum('bhqs,bhsd->bhqd', a.astype(v.dtype), vv))
    return jnp.concatenate(outs, axis=2)

def setup_inputs(seed: int = 0) -> dict:
    key = jax.random.key(seed)
    ks = jax.random.split(key, 10)
    D = D_MODEL
    x = jax.random.normal(ks[0], (BATCH, SEQ, D), jnp.float32)
    rel_bias = 0.5 * jax.random.normal(ks[1], (REL_BUCKETS, N_HEADS), jnp.float32)
    col_scale = jnp.concatenate([jnp.ones((2 * D,), jnp.float32),
                                 jnp.full((D,), DEEPNORM_BETA, jnp.float32)])
    w_qkv = jax.random.normal(ks[2], (DEPTH, D, 3 * D), jnp.float32) * (D ** -0.5) * col_scale
    w_o = jax.random.normal(ks[3], (DEPTH, D, D), jnp.float32) * (D ** -0.5) * DEEPNORM_BETA
    ln_mix_g = 1.0 + 0.02 * jax.random.normal(ks[4], (DEPTH, D), jnp.float32)
    ln_mix_b = 0.02 * jax.random.normal(ks[5], (DEPTH, D), jnp.float32)
    w_up = jax.random.normal(ks[6], (DEPTH, D, D_FF), jnp.float32) * (D ** -0.5) * DEEPNORM_BETA
    w_down = jax.random.normal(ks[7], (DEPTH, D_FF, D), jnp.float32) * (D_FF ** -0.5) * DEEPNORM_BETA
    ln_ffn_g = 1.0 + 0.02 * jax.random.normal(ks[8], (DEPTH, D), jnp.float32)
    ln_ffn_b = 0.02 * jax.random.normal(ks[9], (DEPTH, D), jnp.float32)
    return {"x": x, "rel_bias": rel_bias, "w_qkv": w_qkv, "w_o": w_o,
            "ln_mix_g": ln_mix_g, "ln_mix_b": ln_mix_b, "w_up": w_up, "w_down": w_down,
            "ln_ffn_g": ln_ffn_g, "ln_ffn_b": ln_ffn_b}

def reference(x, rel_bias, w_qkv, w_o, ln_mix_g, ln_mix_b, w_up, w_down, ln_ffn_g, ln_ffn_b):
    B, S, D = x.shape
    h = x
    for i in range(DEPTH):
        qkv = (h @ w_qkv[i]).reshape(B, S, 3, N_HEADS, HEAD_DIM)
        qkv = jnp.transpose(qkv, (2, 0, 3, 1, 4))
        q, k, v = qkv[0], qkv[1], qkv[2]
        if i % N_MIXERS == 0:
            o = moba_attention(q, k, v, rel_bias)
        else:
            o = stick_breaking_attention(q, k, v)
        o = jnp.transpose(o, (0, 2, 1, 3)).reshape(B, S, D) @ w_o[i]
        h = layer_norm(DEEPNORM_ALPHA * h + o, ln_mix_g[i], ln_mix_b[i])
        u = jnp.square(jax.nn.relu(h @ w_up[i]))
        h = layer_norm(DEEPNORM_ALPHA * h + u @ w_down[i], ln_ffn_g[i], ln_ffn_b[i])
    return h


_drawn_inputs = setup_inputs


def setup_inputs(seed=0):
    import zlib

    import numpy as np

    out = dict(_drawn_inputs(seed))
    spreads = {}
    factors = {'rel_bias': 3.674}
    for name, (base, spread) in spreads.items():
        noise = np.random.default_rng([zlib.crc32(name.encode()), seed]).standard_normal(out[name].shape)
        drawn = base * np.exp(spread * noise) if base else spread * noise
        out[name] = __import__('jax').numpy.asarray(drawn.astype(out[name].dtype))
    for name, factor in factors.items():
        out[name] = (out[name] * factor).astype(out[name].dtype)
    return out
```

```python
import math
from contextlib import ExitStack

import numpy as np
import concourse.bass as bass
from concourse import mybir

D = 1024
SEQ = 256
DEPTH = 2
HEADS = 16
DH = D // HEADS
FF = 4 * D
BUCKETS = 32
MAX_DIST = 128
EPS = 1e-5
ALPHA = (2.0 * DEPTH) ** 0.25
QK_SCALE = DH ** -0.5
BIG = 1.0e30

P = 128
TT = SEQ // P
KT = D // P
HG = 4
GROUPS = HEADS // HG
GC = HG * DH
FC = 256
CHUNKS = FF // FC
SLOTS = 4
UNIT = KT * GC
PROJ_UNITS = 3 * GROUPS
ATT_UNITS = PROJ_UNITS + GROUPS
LAYER_UNITS = ATT_UNITS + 2 * CHUNKS
TRIPS = (CHUNKS - 2) // 2
LAST_PAIR = CHUNKS - 2

ACC = 0
PROJ = 0
UP = 4
UP0 = 0
SCORE = 4
PT = 6
OUT = 7
XT = 4

ROWS1 = slice(0, 256)
ROWS0 = slice(256, 384)
SW = 384


def bucket_starts():
    n = np.arange(SEQ)
    exact = BUCKETS // 2
    large = exact + (np.log(np.maximum(n, 1) / exact) / math.log(MAX_DIST / exact)
                     * (BUCKETS - exact)).astype(int)
    b = np.where(n < exact, n, np.minimum(large, BUCKETS - 1))
    return [int(np.argmax(b == i)) for i in range(BUCKETS)] + [SEQ]


def used_before_step(j):
    if j < HEADS - HG:
        return 3 + (3 * j) // HG
    return PROJ_UNITS + max(0, (j - (HEADS - HG)) // 2)


def split_plan():
    plan, done = [], 6
    for j in range(HEADS + 2):
        free = used_before_step(j) + SLOTS - 1
        plan.append(list(range(done, free)))
        done = max(done, free)
    return plan, done


def build(nc, x, rel_bias, w_qkv, w_o, ln_mix_g, ln_mix_b, w_up, w_down, ln_ffn_g, ln_ffn_b, out):
    F32, F32R = mybir.dt.float32, mybir.dt.float32r
    ACT = mybir.ActivationFunctionType
    ALU = mybir.AluOpType
    AX = mybir.AxisListType

    with ExitStack() as ctx:
        def sb(name, shape, dt=F32):
            return ctx.enter_context(nc.sbuf_tensor(name, shape, dt))

        def sem(name):
            return ctx.enter_context(nc.semaphore(name))

        w_raw = sb("w_raw", [P, SLOTS, UNIT])
        w_hi = sb("w_hi", [P, SLOTS, UNIT], F32R)
        w_lo = sb("w_lo", [P, SLOTS, UNIT], F32R)
        h = sb("h", [P, TT, D])
        xT_hi = sb("xT_hi", [P, KT, SEQ], F32R)
        xT_lo = sb("xT_lo", [P, KT, SEQ], F32R)
        xT32 = sb("xT32", [P, 2, SEQ])
        qkv_hi = sb("qkv_hi", [P, 2, 3, 512], F32R)
        qkv_lo = sb("qkv_lo", [P, 2, 3, 512], F32R)
        oT_hi = sb("oT_hi", [P, KT, SEQ], F32R)
        oT_lo = sb("oT_lo", [P, KT, SEQ], F32R)
        bias_rows = sb("bias_rows", [P, HEADS * SEQ])
        z = sb("z", [P, 2, SW])
        p = sb("p", [P, 2, SW])
        cum = sb("cum", [P, SW])
        pT_hi = sb("pT_hi", [P, 2, SW], F32R)
        pT_lo = sb("pT_lo", [P, 2, SW], F32R)
        relu = sb("relu", [P, 2, 512])
        u = sb("u", [P, 512])
        mask = sb("mask", [P, SW])
        ones = sb("ones", [P, SEQ])
        ident = sb("ident", [P, P])
        relT = sb("relT", [HEADS, BUCKETS])
        by_dist = sb("by_dist", [HEADS, SW])
        gb_in = sb("gb_in", [8 * KT, P])
        gbT = sb("gbT", [P, 8 * KT])
        negmax = sb("negmax", [P, 2, 2])
        sums = sb("sums", [P, 2, 2])
        rinv = sb("rinv", [P, 2, 2])
        stats = sb("stats", [P, TT, 2, 6])
        mv = sb("mv", [P, TT, 2])
        veps = sb("veps", [P, TT])
        lnv = sb("lnv", [P, TT])
        rs0 = sb("rs0", [P, TT])
        nt = sb("nt", [P, TT, 2])
        rstd = sb("rstd", [P, TT])
        ps = ctx.enter_context(nc.psum_tensor("ps", [P, 8, 512], F32))
        dist_dram = nc.dram_tensor("dist_dram", (HEADS, SW), F32, kind="Internal")

        bias = bias_rows[:, :].rearrange("p (h k) -> p h k", h=HEADS)
        gb_rows = bias_rows[:, :].rearrange("p (a d) -> p a d", a=4)

        raw_loaded = [sem(f"raw_loaded{s}") for s in range(SLOTS)]
        hi_done = sem("hi_done")
        lo_done = sem("lo_done")
        unit_used = sem("unit_used")
        x_loaded = [sem(f"x_loaded{t}") for t in range(TT)]
        gb_loaded = sem("gb_loaded")
        rel_loaded = sem("rel_loaded")
        dist_stored = sem("dist_stored")
        bias_loaded = sem("bias_loaded")
        rows_loaded = sem("rows_loaded")
        out_stored = sem("out_stored")
        const_ready = sem("const_ready")
        pool_own = sem("pool_own")
        dve_own = sem("dve_own")
        act_own = sem("act_own")
        gbT_psum = sem("gbT_psum")
        gbT_ready = sem("gbT_ready")
        xhat_ready = sem("xhat_ready")
        xT_psum = sem("xT_psum")
        xT_act = sem("xT_act")
        xT_ready = sem("xT_ready")
        h_ready = sem("h_ready")
        var_ready = sem("var_ready")
        rs0_ready = sem("rs0_ready")
        qkv_hi_ready = sem("qkv_hi_ready")
        qkv_ready = sem("qkv_ready")
        score_done = sem("score_done")
        z_ready = sem("z_ready")
        logit_ready = sem("logit_ready")
        soft_done = sem("soft_done")
        exp_done = sem("exp_done")
        prob_ready = sem("prob_ready")
        pT_psum = sem("pT_psum")
        pT_hi_ready = sem("pT_hi_ready")
        pT_ready = sem("pT_ready")
        pv_done = sem("pv_done")
        oT_hi_ready = sem("oT_hi_ready")
        oT_ready = sem("oT_ready")
        relu_ready = sem("relu_ready")
        uT_ready = sem("uT_ready")
        acc_done = sem("acc_done")
        y_ready = [sem(f"y_ready{t}") for t in range(TT)]

        def f32(ap):
            return ap.bitcast(F32)

        class Own:
            def __init__(self, s):
                self.s, self.n, self.shift = s, 0, 0

            def mark(self, ins):
                ins.then_inc(self.s, 1)
                self.n += 1

            def wait(self, eng):
                eng.wait_ge(self.s, self.n + self.shift)

        def uT(t, c):
            return t[:, c % 2, 0, :].rearrange("p (k s) -> p k s", k=FC // P)

        SPLITS, SPLIT_DONE = split_plan()
        A_STEPS = HEADS + 2
        block = ctx.enter_context(nc.Block())

        @block.sync
        def _(sp):
            for t in range(TT):
                sp.dma_start(h[:, t, :], x[0, t * P:(t + 1) * P, :]).then_inc(x_loaded[t], 16)

            def load(n, slot, src, shape, always=False):
                if always or n >= SLOTS:
                    sp.wait_ge(lo_done, n - SLOTS + 1)
                dst = w_raw[:, slot, :].rearrange("p (k n) -> p k n", k=shape)
                sp.dma_start(dst, src).then_inc(raw_loaded[slot], 16)

            for l in range(DEPTH):
                n0 = l * LAYER_UNITS
                qkv_l = w_qkv[l].rearrange("(k p) (w n) -> p k w n", p=P, w=3)
                o_l = w_o[l].rearrange("(g k p) n -> p g k n", p=P, g=GROUPS)
                up_l = w_up[l].rearrange("(k p) n -> p k n", p=P)
                down_l = w_down[l].rearrange("(k p) n -> p k n", p=P)
                for m in range(PROJ_UNITS):
                    g, w = divmod(m, 3)
                    load(n0 + m, m % SLOTS, qkv_l[:, :, w, g * GC:(g + 1) * GC], KT)
                for g in range(GROUPS):
                    m = PROJ_UNITS + g
                    load(n0 + m, m % SLOTS, o_l[:, g], GC // P)

                def load_up(n, slot, c):
                    load(n, slot, up_l[:, :, bass.ds(c * FC, FC)], KT, True)

                def load_down(n, slot, c):
                    load(n, slot, down_l[:, bass.ds(c * (FC // P), FC // P), :], FC // P, True)

                f0 = n0 + ATT_UNITS
                load_up(f0, 0, 0)
                with sp.Fori(0, TRIPS) as i:
                    load_up(f0 + 1 + 4 * i, 1, 2 * i + 1)
                    load_down(f0 + 2 + 4 * i, 2, 2 * i)
                    load_up(f0 + 3 + 4 * i, 3, 2 * i + 2)
                    load_down(f0 + 4 + 4 * i, 0, 2 * i + 1)
                load_up(f0 + 29, 1, CHUNKS - 1)
                load_down(f0 + 30, 2, CHUNKS - 2)
                load_down(f0 + 31, 3, CHUNKS - 1)

            for t in range(TT):
                sp.wait_ge(y_ready[t], 1)
                sp.dma_start(out[0, t * P:(t + 1) * P, :], h[:, t, :]).then_inc(out_stored, 16)
            sp.wait_ge(out_stored, 16 * TT)

        @block.gpsimd
        def _(pool):
            own = Own(pool_own)
            own.mark(pool.memset(ident[:, :], 0.0))
            own.mark(pool.memset(mask[:, :], 0.0))
            own.mark(pool.memset(by_dist[:, :], -BIG))
            pool.memset(ones[:, :], 1.0).then_inc(const_ready, 1)
            pool.dma_start(relT[:, :], rel_bias.rearrange("b h -> h b"),
                           allow_slow_non_contiguous=True).then_inc(rel_loaded, 16)
            own.wait(pool)
            pool.affine_select(out=ident[:, :], in_=ident[:, :], compare_op=ALU.not_equal, fill=1.0,
                               base=0, pattern=[[-1, P]], channel_multiplier=1).then_inc(const_ready, 1)
            diag = mask[:, P:SW].rearrange("p (a k) -> p a k", a=2)
            pool.affine_select(out=diag, in_=diag, compare_op=ALU.is_gt, fill=-BIG,
                               base=0, pattern=[[0, 2], [-1, P]], channel_multiplier=1).then_inc(const_ready, 1)
            pool.wait_ge(rel_loaded, 16)
            starts = bucket_starts()
            exact = BUCKETS // 2
            own.mark(pool.tensor_copy(by_dist[:, P - 1:P - 1 + exact], relT[:, 0:exact]))
            for b in range(exact, BUCKETS):
                lo, hi = starts[b], starts[b + 1]
                own.mark(pool.tensor_copy(by_dist[:, P - 1 + lo:P - 1 + hi],
                                          relT[:, b:b + 1].to_broadcast([HEADS, hi - lo])))
            own.wait(pool)
            pool.dma_start(dist_dram.ap(), by_dist[:, :]).then_inc(dist_stored, 16)
            pool.wait_ge(dist_stored, 16)
            pool.dma_start(bias, bass.AP(dist_dram, 0, [[1, P], [SW, HEADS], [1, SEQ]])).then_inc(bias_loaded, 16)

            for l in range(DEPTH):
                if l == 0:
                    pool.wait_ge(z_ready, HEADS)
                else:
                    pool.wait_ge(h_ready, 2 * TT)
                for a, v in enumerate((ln_mix_g, ln_mix_b, ln_ffn_g, ln_ffn_b)):
                    pool.dma_start(gb_rows[:, a, :], bass.AP(v.tensor, l * D, [[0, P], [1, D]])).then_inc(rows_loaded, 16)
                pool.wait_ge(rows_loaded, 64 * (l + 1))
                for s in range(2):
                    ln = 2 * l + s + 1
                    if ln == 2 * DEPTH:
                        break
                    pool.wait_ge(xT_psum, 4 * (ln + 1))
                    for t in range(TT):
                        own.mark(pool.tensor_tensor(h[:, t, :], h[:, t, :], gb_rows[:, 2 * s, :], ALU.mult))
                        own.wait(pool)
                        pool.tensor_tensor(h[:, t, :], h[:, t, :], gb_rows[:, 2 * s + 1, :],
                                           ALU.add).then_inc(h_ready, 1)
            pool.wait_ge(xhat_ready, 4 * (2 * DEPTH - 1) + 2)
            own.mark(pool.tensor_tensor(h[:, 0, :], h[:, 0, :], gb_rows[:, 2, :], ALU.mult))
            own.wait(pool)
            pool.tensor_tensor(h[:, 0, :], h[:, 0, :], gb_rows[:, 3, :], ALU.add).then_inc(y_ready[0], 1)

        @block.scalar
        def _(act):
            own = Own(act_own)
            act.preload_act_table_set("natural_log_exp_and_others")
            for a, v in enumerate((ln_mix_g, ln_mix_b, ln_ffn_g, ln_ffn_b)):
                act.dma_start(gb_in[a * 2 * KT:(a + 1) * 2 * KT, :],
                              v.rearrange("l (k p) -> (l k) p", p=P)).then_inc(gb_loaded, 16)

            def split_hi(n, slot, always=False, uses=None):
                act.wait_ge(raw_loaded[slot], uses if uses is not None else 16 * (n // SLOTS + 1))
                if always or n >= SLOTS:
                    act.wait_ge(unit_used, n - SLOTS + 1)
                act.copy(w_hi[:, slot, :], w_raw[:, slot, :]).then_inc(hi_done, 1)

            def xT_evac(ln):
                for k in range(KT):
                    if k % 2 == 0:
                        act.wait_ge(xT_psum, 4 * ln + k // 2 + 1)
                    if k >= 2 or ln >= 1:
                        act.wait_ge(xT_ready, 8 * ln + k - 1)
                    src = ps[:, XT + k // 2, (k % 2) * SEQ:(k % 2 + 1) * SEQ]
                    if ln == 0:
                        act.copy(xT_hi[:, k, :], src)
                        act.copy(xT32[:, k % 2, :], src).then_inc(xT_act, 1)
                    else:
                        if ln == 1 and k == 0:
                            act.wait_ge(gbT_ready, 1)
                        l, s = divmod(ln - 1, 2)
                        col = 4 * s * KT + l * KT + k
                        gain, offs = gbT[:, col:col + 1], gbT[:, col + 2 * KT:col + 2 * KT + 1]
                        act.activation(xT_hi[:, k, :], src, ACT.Identity, bias=offs, scale=gain)
                        act.activation(xT32[:, k % 2, :], src, ACT.Identity, bias=offs, scale=gain).then_inc(xT_act, 1)

            def ln_rstd(ln):
                for t in range(TT):
                    act.wait_ge(var_ready, TT * (ln - 1) + t + 1)
                    own.mark(act.activation(lnv[:, t:t + 1], veps[:, t:t + 1], ACT.Ln))
                    own.wait(act)
                    act.activation(rs0[:, t:t + 1], lnv[:, t:t + 1], ACT.Exp, scale=-0.5).then_inc(rs0_ready, 1)

            def qkv_evac(l, g, w):
                m = 3 * g + w
                act.wait_ge(unit_used, LAYER_UNITS * l + m + 1)
                if g >= 2:
                    act.wait_ge(pv_done, HEADS * l + HG * (g - 1))
                act.activation(qkv_hi[:, g % 2, w, :], ps[:, PROJ + m % 2, :], ACT.Copy,
                               scale=QK_SCALE if w == 0 else 1.0).then_inc(qkv_hi_ready, 1)

            def exp_part(l, j):
                hd = HEADS * l + j
                zj, pj = z[:, j % 2, :], p[:, j % 2, :]
                act.wait_ge(logit_ready, hd + 1)
                if l == 0:
                    if j >= 2:
                        act.wait_ge(pT_psum, hd - 1)
                    act.activation(pj[:, ROWS1], zj[:, ROWS1], ACT.Exp, bias=negmax[:, j % 2, 0:1],
                                   accum_out=sums[:, j % 2, 0:1])
                    act.activation(pj[:, ROWS0], zj[:, ROWS0], ACT.Exp, bias=negmax[:, j % 2, 1:2],
                                   accum_out=sums[:, j % 2, 1:2]).then_inc(exp_done, 1)
                else:
                    act.activation(pj, zj, ACT.Exp).then_inc(exp_done, 1)

            def softplus_part(l, j):
                hd = HEADS * l + j
                zj, pj = z[:, j % 2, :], p[:, j % 2, :]
                act.wait_ge(z_ready, hd + 1)
                act.wait_ge(pT_psum, hd - 1)
                own.mark(act.activation(pj, zj, ACT.Abs))
                own.wait(act)
                own.mark(act.activation(pj, pj, ACT.Exp, scale=-1.0))
                own.wait(act)
                act.activation(pj, pj, ACT.Ln, bias=1.0).then_inc(soft_done, 1)

            def pT_evac(l, j):
                hd = HEADS * l + j
                act.wait_ge(pT_psum, hd + 1)
                if j >= 2:
                    act.wait_ge(pv_done, hd - 1)
                act.copy(pT_hi[:, j % 2, :], ps[:, PT, 0:SW]).then_inc(pT_hi_ready, 1)

            def o_evac(l, j):
                hd = HEADS * l + j
                rows = slice(DH * (j % 2), DH * (j % 2) + DH)
                act.wait_ge(pv_done, hd + 1)
                act.copy(oT_hi[rows, j // 2, :], ps[rows, OUT, 0:SEQ]).then_inc(oT_hi_ready, 1)

            def relu_evac(k, l, c, first=False):
                act.wait_ge(unit_used, LAYER_UNITS * l + ATT_UNITS + (1 if first else 2 * c))
                if not first:
                    act.wait_ge(uT_ready, CHUNKS * l + c)
                act.activation(relu[:, k, :], ps[:, UP0 if first else UP + k, :], ACT.Relu).then_inc(relu_ready, 1)

            for n in range(3):
                split_hi(n, n)
            xT_evac(0)
            split_hi(3, 3)
            for l in range(DEPTH):
                n0 = l * LAYER_UNITS
                qkv_evac(l, 0, 0)
                split_hi(n0 + 4, 0)
                qkv_evac(l, 0, 1)
                split_hi(n0 + 5, 1)
                qkv_evac(l, 0, 2)
                evac = 3
                for j in range(A_STEPS):
                    for m in SPLITS[j]:
                        split_hi(n0 + m, m % SLOTS)
                    if j < HEADS:
                        if l == 0:
                            exp_part(l, j)
                        else:
                            softplus_part(l, j)
                    if 1 <= j <= HEADS:
                        pT_evac(l, j - 1)
                    if 2 <= j:
                        o_evac(l, j - 2)
                    if j < HEADS and l == 1:
                        exp_part(l, j)
                    while evac < min(PROJ_UNITS, used_before_step(j + 1)):
                        qkv_evac(l, evac // 3, evac % 3)
                        evac += 1
                for m in range(SPLIT_DONE, ATT_UNITS + 3):
                    split_hi(n0 + m, m % SLOTS)
                ln_rstd(2 * l + 1)
                xT_evac(2 * l + 1)

                f0 = n0 + ATT_UNITS
                relu_evac(0, l, 0, first=True)
                r0 = 16 * (f0 // SLOTS)
                with act.Fori(0, TRIPS) as i:
                    split_hi(f0 + 3 + 4 * i, 3, True, r0 + 16 + 16 * i)
                    split_hi(f0 + 4 + 4 * i, 0, True, r0 + 32 + 16 * i)
                    relu_evac(1, l, 2 * i + 1)
                    split_hi(f0 + 5 + 4 * i, 1, True, r0 + 32 + 16 * i)
                    split_hi(f0 + 6 + 4 * i, 2, True, r0 + 32 + 16 * i)
                    relu_evac(0, l, 2 * i + 2)
                split_hi(f0 + 31, 3)
                if l + 1 < DEPTH:
                    split_hi(f0 + 32, 0)
                relu_evac(1, l, CHUNKS - 1)
                if l + 1 < DEPTH:
                    split_hi(f0 + 33, 1)
                    split_hi(f0 + 34, 2)
                ln_rstd(2 * l + 2)
                if l + 1 < DEPTH:
                    xT_evac(2 * l + 2)
                    split_hi(f0 + 35, 3)

        @block.vector
        def _(dve):
            own = Own(dve_own)

            def split_lo(n, slot):
                dve.wait_ge(hi_done, n + 1)
                dve.tensor_tensor(w_lo[:, slot, :], w_raw[:, slot, :], f32(w_hi[:, slot, :]),
                                  ALU.subtract).then_inc(lo_done, 1)

            def xT_evac(ln):
                for k in range(KT):
                    dve.wait_ge(xT_act, 8 * ln + k + 1)
                    dve.tensor_tensor(xT_lo[:, k, :], xT32[:, k % 2, :], f32(xT_hi[:, k, :]),
                                      ALU.subtract).then_inc(xT_ready, 1)

            def norm(ln):
                def add_and_measure(t, s):
                    hs = h[:, t, s * 512:(s + 1) * 512]
                    if t == 0 and s == 0 and ln >= 2:
                        dve.wait_ge(h_ready, TT * (ln - 1))
                    if 2 * t + s < 3:
                        dve.wait_ge(acc_done, 3 * (ln - 1) + 2 * t + s + 1)
                    else:
                        l, ffn = divmod(ln - 1, 2)
                        dve.wait_ge(unit_used, LAYER_UNITS * l + (LAYER_UNITS if ffn else ATT_UNITS))
                    own.mark(dve.scalar_tensor_tensor(hs, hs, ALPHA, ps[:, ACC + 2 * t + s, :],
                                                      ALU.mult, ALU.add))
                    own.wait(dve)
                    own.mark(dve.bn_stats(stats[:, t, s, :], hs))

                def variance(t):
                    own.wait(dve)
                    own.mark(dve.bn_aggr(mv[:, t, :], stats[:, t, :, :]))
                    own.wait(dve)
                    dve.tensor_scalar(veps[:, t:t + 1], mv[:, t, 1:2], EPS, None,
                                      ALU.add).then_inc(var_ready, 1)

                def centre_and_scale(t):
                    dve.wait_ge(rs0_ready, TT * (ln - 1) + t + 1)
                    r0, v = rs0[:, t:t + 1], veps[:, t:t + 1]
                    own.mark(dve.scalar_tensor_tensor(nt[:, t, 0:1], r0, v, r0, ALU.mult, ALU.mult))
                    own.wait(dve)
                    own.mark(dve.tensor_scalar(nt[:, t, 1:2], nt[:, t, 0:1], -0.5, 1.5, ALU.mult, ALU.add))
                    own.wait(dve)
                    own.mark(dve.tensor_tensor(rstd[:, t:t + 1], r0, nt[:, t, 1:2], ALU.mult))
                    own.wait(dve)
                    for s in range(2):
                        hs = h[:, t, s * 512:(s + 1) * 512]
                        dve.tensor_scalar(hs, hs, mv[:, t, 0:1], rstd[:, t:t + 1],
                                          ALU.subtract, ALU.mult).then_inc(xhat_ready, 1)

                add_and_measure(0, 0)
                add_and_measure(0, 1)
                variance(0)
                add_and_measure(1, 0)
                centre_and_scale(0)
                add_and_measure(1, 1)
                variance(1)
                centre_and_scale(1)

            def qkv_evac(l, g, w):
                m = 3 * g + w
                dve.wait_ge(qkv_hi_ready, PROJ_UNITS * l + m + 1)
                dve.scalar_tensor_tensor(qkv_lo[:, g % 2, w, :], ps[:, PROJ + m % 2, :],
                                         QK_SCALE if w == 0 else 1.0, f32(qkv_hi[:, g % 2, w, :]),
                                         ALU.mult, ALU.subtract).then_inc(qkv_ready, 1)

            def scores(l, j):
                hd = HEADS * l + j
                s, zj = ps[:, SCORE + j % 2, 0:SW], z[:, j % 2, :]
                dve.wait_ge(score_done, hd + 1)
                if hd >= 2:
                    dve.wait_ge(exp_done, hd - 1)
                if l == 0:
                    if j == 0:
                        dve.wait_ge(bias_loaded, 16)
                    rev = bass.AP(bias_rows, j * SEQ + SEQ - 1, [[HEADS * SEQ, P], [-1, SEQ]])
                    rev0 = bass.AP(bias_rows, j * SEQ + P - 1, [[HEADS * SEQ, P], [-1, P]])
                    own.mark(dve.scalar_tensor_tensor(zj[:, ROWS1], s[:, ROWS1], 1.0, rev, ALU.mult, ALU.add))
                    dve.scalar_tensor_tensor(zj[:, ROWS0], s[:, ROWS0], 1.0, rev0, ALU.mult,
                                             ALU.add).then_inc(z_ready, 1)
                    own.wait(dve)
                    dve.reduce_max(negmax[:, j % 2, 0:1], zj[:, ROWS1], AX.X, negate=True)
                    dve.wait_ge(z_ready, hd + 1)
                    dve.reduce_max(negmax[:, j % 2, 1:2], zj[:, ROWS0], AX.X, negate=True).then_inc(logit_ready, 1)
                else:
                    if j == 0:
                        dve.wait_ge(const_ready, 3)
                    dve.scalar_tensor_tensor(zj, s, 1.0, mask[:, :], ALU.mult, ALU.add).then_inc(z_ready, 1)

            def normalise(l, j):
                hd = HEADS * l + j
                dve.wait_ge(exp_done, hd + 1)
                own.mark(dve.reciprocal(rinv[:, j % 2, :], sums[:, j % 2, :]))
                own.wait(dve)
                for i, rows in enumerate((ROWS1, ROWS0)):
                    pj = p[:, j % 2, rows]
                    dve.tensor_scalar(pj, pj, rinv[:, j % 2, i:i + 1], None, ALU.mult).then_inc(prob_ready, 1)

            def stick(l, j):
                hd = HEADS * l + j
                zj, pj = z[:, j % 2, :], p[:, j % 2, :]
                dve.wait_ge(soft_done, j + 1)
                own.mark(dve.scalar_tensor_tensor(pj, zj, 0.0, pj, ALU.max, ALU.add))
                own.wait(dve)
                for rows in (ROWS1, ROWS0):
                    n = rows.stop - rows.start
                    back = bass.AP(p, (j % 2) * SW + rows.stop - 1, [[2 * SW, P], [-1, n]])
                    back_sum = bass.AP(cum, rows.stop - 1, [[SW, P], [-1, n]])
                    own.mark(dve.tensor_tensor_scan(back_sum, ones[:, 0:n], back, 0.0, ALU.mult, ALU.add))
                own.wait(dve)
                dve.tensor_tensor(zj, zj, cum[:, :], ALU.subtract).then_inc(logit_ready, 1)

            def pT_evac(l, j):
                hd = HEADS * l + j
                dve.wait_ge(pT_hi_ready, hd + 1)
                dve.tensor_tensor(pT_lo[:, j % 2, :], ps[:, PT, 0:SW], f32(pT_hi[:, j % 2, :]),
                                  ALU.subtract).then_inc(pT_ready, 1)

            def o_evac(l, j):
                hd = HEADS * l + j
                rows = slice(DH * (j % 2), DH * (j % 2) + DH)
                dve.wait_ge(oT_hi_ready, hd + 1)
                dve.tensor_tensor(oT_lo[rows, j // 2, :], ps[rows, OUT, 0:SEQ], f32(oT_hi[rows, j // 2, :]),
                                  ALU.subtract).then_inc(oT_ready, 1)

            def square(k, l, c):
                dve.wait_ge(relu_ready, CHUNKS * l + c + 1)
                own.mark(dve.tensor_tensor(u[:, :], relu[:, k, :], relu[:, k, :], ALU.mult))
                own.wait(dve)
                own.mark(dve.tensor_copy(qkv_hi[:, k, 0, :], u[:, :]))
                own.wait(dve)
                dve.tensor_tensor(qkv_lo[:, k, 0, :], u[:, :], f32(qkv_hi[:, k, 0, :]),
                                  ALU.subtract).then_inc(uT_ready, 1)

            dve.wait_ge(gbT_psum, 1)
            dve.tensor_copy(gbT[:, :], ps[:, PROJ, 0:8 * KT]).then_inc(gbT_ready, 1)
            for n in range(3):
                split_lo(n, n)
            xT_evac(0)
            split_lo(3, 3)
            for l in range(DEPTH):
                n0 = l * LAYER_UNITS
                qkv_evac(l, 0, 0)
                split_lo(n0 + 4, 0)
                qkv_evac(l, 0, 1)
                split_lo(n0 + 5, 1)
                qkv_evac(l, 0, 2)
                evac = 3
                for j in range(A_STEPS):
                    if j < HEADS:
                        scores(l, j)
                    for m in SPLITS[j]:
                        split_lo(n0 + m, m % SLOTS)
                    if 1 <= j <= HEADS:
                        pT_evac(l, j - 1)
                    if j < HEADS:
                        normalise(l, j) if l == 0 else stick(l, j)
                    if 2 <= j:
                        o_evac(l, j - 2)
                    while evac < min(PROJ_UNITS, used_before_step(j + 1)):
                        qkv_evac(l, evac // 3, evac % 3)
                        evac += 1
                for m in range(SPLIT_DONE, ATT_UNITS + 3):
                    split_lo(n0 + m, m % SLOTS)
                norm(2 * l + 1)
                xT_evac(2 * l + 1)

                f0 = n0 + ATT_UNITS
                square(0, l, 0)
                per_trip, start = 4, own.n
                with dve.Fori(0, TRIPS) as i:
                    own.shift = per_trip * i
                    split_lo(f0 + 3 + 4 * i, 3)
                    split_lo(f0 + 4 + 4 * i, 0)
                    square(1, l, 2 * i + 1)
                    split_lo(f0 + 5 + 4 * i, 1)
                    split_lo(f0 + 6 + 4 * i, 2)
                    square(0, l, 2 * i + 2)
                assert own.n == start + per_trip
                own.n, own.shift = start + per_trip * TRIPS, 0
                split_lo(f0 + 31, 3)
                if l + 1 < DEPTH:
                    split_lo(f0 + 32, 0)
                square(1, l, CHUNKS - 1)
                if l + 1 < DEPTH:
                    split_lo(f0 + 33, 1)
                    split_lo(f0 + 34, 2)
                norm(2 * l + 2)
                if l + 1 < DEPTH:
                    xT_evac(2 * l + 2)
                    split_lo(f0 + 35, 3)
            dve.wait_ge(rows_loaded, 64 * DEPTH)
            dve.wait_ge(xhat_ready, 4 * 2 * DEPTH)
            own.mark(dve.tensor_tensor(h[:, 1, :], h[:, 1, :], gb_rows[:, 2, :], ALU.mult))
            own.wait(dve)
            dve.tensor_tensor(h[:, 1, :], h[:, 1, :], gb_rows[:, 3, :], ALU.add).then_inc(y_ready[1], 1)

        @block.tensor
        def _(pe):
            PASSES = ((0, 0), (0, 1), (1, 0))
            xT, w, qkv, oT, pT = (xT_hi, xT_lo), (w_hi, w_lo), (qkv_hi, qkv_lo), (oT_hi, oT_lo), (pT_hi, pT_lo)

            def transposes(ln):
                for t in range(TT):
                    for k in range(KT):
                        if ln == 0 and k == 0:
                            pe.wait_ge(x_loaded[t], 16)
                        if ln >= 1 and k % 4 == 0:
                            pe.wait_ge(xhat_ready, 4 * (ln - 1) + 2 * t + k // 4 + 1)
                        o = (k % 2) * SEQ + t * P
                        mm = pe.transpose(ps[:, XT + k // 2, o:o + P], h[:, t, k * P:(k + 1) * P], ident[:, :])
                        if t == TT - 1 and k % 2 == 1:
                            mm.then_inc(xT_psum, 1)

            def feature_major(slot, bank, k, ln):
                wk = [t[:, slot, :].rearrange("p (k n) -> p k n", k=KT) for t in w]
                if ln is not None:
                    pe.wait_ge(xT_ready, 8 * ln + k + 1)
                for c in range(2):
                    for i, (a, b) in enumerate(PASSES):
                        mm = pe.matmul(ps[:, bank, c * SEQ:(c + 1) * SEQ], wk[a][:, k, c * P:(c + 1) * P],
                                       xT[b][:, k, :], start=(k == 0 and c == 0 and i == 0),
                                       stop=(k == KT - 1 and i == 2), skip_group_check=True)
                return mm

            def token_major(slot, bank, k):
                wk = [t[:, slot, :].rearrange("p (k n) -> p k n", k=KT) for t in w]
                for t in range(TT):
                    for i, (a, b) in enumerate(PASSES):
                        mm = pe.matmul(ps[:, bank, t * GC:(t + 1) * GC], xT[a][:, k, t * P:(t + 1) * P],
                                       wk[b][:, k, :], start=(k == 0 and t == 0 and i == 0),
                                       stop=(k == KT - 1 and i == 2), skip_group_check=True)
                return mm

            def proj(l, m, k):
                g, which = divmod(m, 3)
                n = l * LAYER_UNITS + m
                if k == 0:
                    pe.wait_ge(lo_done, n + 1)
                    if m >= 2:
                        pe.wait_ge(qkv_ready, PROJ_UNITS * l + m - 1)
                if which < 2:
                    mm = feature_major(m % SLOTS, PROJ + m % 2, k, 2 * l if m == 0 else None)
                else:
                    mm = token_major(m % SLOTS, PROJ + m % 2, k)
                if k == KT - 1:
                    mm.then_inc(unit_used, 1)

            def sum_part(slot, src, k_src, k, t, first, last, halves=(0, 1)):
                wk = [x[:, slot, :].rearrange("p (k n) -> p k n", k=FC // P) for x in w]
                for s in halves:
                    for i, (a, b) in enumerate(PASSES):
                        mm = pe.matmul(ps[:, ACC + 2 * t + s, :], src[a][:, k_src, t * P:(t + 1) * P],
                                       wk[b][:, k, s * 512:(s + 1) * 512],
                                       start=(first and i == 0), stop=(last and i == 2))
                return mm

            def o_slice(l, q):
                g, r = divmod(q, 4)
                k, t = divmod(r, 2)
                n = l * LAYER_UNITS + PROJ_UNITS + g
                if r == 0:
                    pe.wait_ge(lo_done, n + 1)
                    pe.wait_ge(oT_ready, HEADS * l + HG * (g + 1))
                    if g == 0:
                        pe.wait_ge(qkv_ready, PROJ_UNITS * (l + 1))
                mm = sum_part((PROJ_UNITS + g) % SLOTS, oT, 2 * g + k, k, t, q < 2, False)
                if r == 3:
                    mm.then_inc(unit_used, 1)

            def last_unit(slot, src, k0):
                for t in range(TT):
                    for s in range(2):
                        for k in range(2):
                            mm = sum_part(slot, src, k0 + k, k, t, False, k == 1, halves=(s,))
                        if 2 * t + s < 3:
                            mm.then_inc(acc_done, 1)
                mm.then_inc(unit_used, 1)

            def attend_scores(l, j):
                hd = HEADS * l + j
                par, tile, r0 = (j // HG) % 2, (j % HG) // 2, DH * (j % 2)
                if j % HG == 0:
                    pe.wait_ge(qkv_ready, PROJ_UNITS * l + 3 * (j // HG) + 3)
                if j >= 2:
                    pe.wait_ge(z_ready, hd - 1)
                q = [t[r0:r0 + DH, par, 0, tile * SEQ:(tile + 1) * SEQ] for t in qkv]
                kk = [t[r0:r0 + DH, par, 1, tile * SEQ:(tile + 1) * SEQ] for t in qkv]
                for cols, t, nk in ((ROWS1, 1, SEQ), (ROWS0, 0, P)):
                    for i, (a, b) in enumerate(PASSES):
                        mm = pe.matmul(ps[:, SCORE + j % 2, cols], q[a][:, t * P:(t + 1) * P], kk[b][:, 0:nk],
                                       start=(i == 0), stop=(i == 2))
                mm.then_inc(score_done, 1)

            def attend_transpose(l, j):
                hd = HEADS * l + j
                if l == 0:
                    pe.wait_ge(prob_ready, 2 * (j + 1))
                else:
                    pe.wait_ge(exp_done, hd + 1)
                if hd >= 1:
                    pe.wait_ge(pT_ready, hd)
                pj = p[:, j % 2, :]
                for dst, src in ((0, 256), (128, 0), (256, 128)):
                    mm = pe.transpose(ps[:, PT, dst:dst + P], pj[:, src:src + P], ident[:, :])
                mm.then_inc(pT_psum, 1)

            def attend_values(l, j):
                hd = HEADS * l + j
                par, pair = (j // HG) % 2, (j % HG) // 2
                pe.wait_ge(pT_ready, hd + 1)
                if hd >= 1:
                    pe.wait_ge(oT_ready, hd)
                for kt, dst, src in ((0, slice(0, SEQ), slice(0, SEQ)), (1, slice(P, SEQ), slice(SEQ, SW))):
                    for i, (a, b) in enumerate(PASSES):
                        v = qkv[a][:, par, 2, kt * GC + pair * P:kt * GC + (pair + 1) * P]
                        mm = pe.matmul(ps[:, OUT, dst], v, pT[b][:, j % 2, src],
                                       start=(kt == 0 and i == 0), stop=(kt == 1 and i == 2))
                mm.then_inc(pv_done, 1)

            def up(l, c, n, slot, bank, ln=None, wait_bank=True):
                pe.wait_ge(lo_done, n + 1)
                if wait_bank:
                    pe.wait_ge(relu_ready, CHUNKS * l + c - 1)
                for k in range(KT):
                    mm = feature_major(slot, bank, k, ln)
                mm.then_inc(unit_used, 1)

            def down(l, c, n, slot, par, first=False):
                pe.wait_ge(lo_done, n + 1)
                pe.wait_ge(uT_ready, CHUNKS * l + c + 1)
                src = [uT(t, par) for t in qkv]
                for k in range(2):
                    for t in range(TT):
                        mm = sum_part(slot, src, k, k, t, first and k == 0, False)
                mm.then_inc(unit_used, 1)

            pe.wait_ge(const_ready, 3)
            pe.wait_ge(gb_loaded, 64)
            pe.transpose(ps[:, PROJ, 0:8 * KT], gb_in[:, :], ident[0:8 * KT, 0:8 * KT]).then_inc(gbT_psum, 1)
            for l in range(DEPTH):
                transposes(2 * l)
                if l == 0:
                    pe.wait_ge(gbT_ready, 1)
                for m in range(3):
                    for k in range(KT):
                        proj(l, m, k)
                ksteps = iter([(m, k) for m in range(3, PROJ_UNITS) for k in range(KT)])
                slices = iter(range(4 * (GROUPS - 1)))
                for j in range(A_STEPS):
                    def fill():
                        if j < HEADS - HG:
                            for _ in range(2):
                                proj(l, *next(ksteps))
                        else:
                            q = next(slices, None)
                            if q is not None:
                                o_slice(l, q)
                    fill()
                    if j < HEADS:
                        attend_scores(l, j)
                    fill()
                    if 1 <= j <= HEADS:
                        attend_transpose(l, j - 1)
                    if j < HEADS - HG:
                        fill()
                    if j >= 2:
                        attend_values(l, j - 2)
                n = l * LAYER_UNITS + ATT_UNITS - 1
                pe.wait_ge(lo_done, n + 1)
                pe.wait_ge(oT_ready, HEADS * (l + 1))
                last_unit((ATT_UNITS - 1) % SLOTS, oT, KT - 2)

                transposes(2 * l + 1)
                f0 = l * LAYER_UNITS + ATT_UNITS
                up(l, 0, f0, 0, UP0, ln=2 * l + 1, wait_bank=False)
                up(l, 1, f0 + 1, 1, UP + 1, wait_bank=False)
                down(l, 0, f0 + 2, 2, 0, first=True)
                up(l, 2, f0 + 3, 3, UP)
                down(l, 1, f0 + 4, 0, 1)
                with pe.Fori(1, TRIPS) as i:
                    up(l, 2 * i + 1, f0 + 1 + 4 * i, 1, UP + 1)
                    down(l, 2 * i, f0 + 2 + 4 * i, 2, 0)
                    up(l, 2 * i + 2, f0 + 3 + 4 * i, 3, UP)
                    down(l, 2 * i + 1, f0 + 4 + 4 * i, 0, 1)
                up(l, CHUNKS - 1, f0 + 29, 1, UP + 1)
                down(l, CHUNKS - 2, f0 + 30, 2, 0)
                pe.wait_ge(lo_done, f0 + 32)
                pe.wait_ge(uT_ready, CHUNKS * (l + 1))
                last_unit(3, [uT(t, 1) for t in qkv], 0)


INS = ["x", "rel_bias", "w_qkv", "w_o", "ln_mix_g", "ln_mix_b", "w_up", "w_down", "ln_ffn_g", "ln_ffn_b"]


def kernel(**inputs):
    import numpy as _np
    import concourse.bacc as _bacc
    from concourse import mybir as _mybir
    from concourse.bass_utils import run_bass_kernel_spmd as _run

    nc = _bacc.Bacc("TRN2", target_bir_lowering=False, num_devices=1)
    arrays, args = {}, []
    for name in INS:
        a = _np.ascontiguousarray(inputs[name])
        arrays[f"in_{name}_dram"] = a
        args.append(nc.dram_tensor(f"in_{name}_dram", a.shape, _mybir.dt.from_np(a.dtype), kind="ExternalInput").ap())
    args.append(nc.dram_tensor("out_0_dram", (1, SEQ, D), _mybir.dt.float32, kind="ExternalOutput").ap())
    build(nc, *args)
    r = _run(nc, [arrays], core_ids=[0])
    return r.results[0]["out_0_dram"]
```

```python
import math
from contextlib import ExitStack

import numpy as np
import concourse.bass as bass
from concourse import mybir

D = 1024
SEQ = 256
DEPTH = 2
HEADS = 16
DH = D // HEADS
FF = 4 * D
BUCKETS = 32
MAX_DIST = 128
EPS = 1e-5
ALPHA = (2.0 * DEPTH) ** 0.25
QK_SCALE = DH ** -0.5
BIG = 1.0e30

P = 128
TT = SEQ // P
KT = D // P
HG = 4
GROUPS = HEADS // HG
GC = HG * DH
FC = 256
CHUNKS = FF // FC
SLOTS = 4
UNIT = KT * GC
PROJ_UNITS = 3 * GROUPS
ATT_UNITS = PROJ_UNITS + GROUPS
LAYER_UNITS = ATT_UNITS + 2 * CHUNKS
TRIPS = (CHUNKS - 2) // 2

ACC = 0
PROJ = 2
UP = 4
UP0 = 0
SCORE = 4
PT = 6
OUT = 7
XT = 4

ROWS1 = slice(0, 256)
ROWS0 = slice(256, 384)
SW = 384


def bucket_starts():
    n = np.arange(SEQ)
    exact = BUCKETS // 2
    large = exact + (np.log(np.maximum(n, 1) / exact) / math.log(MAX_DIST / exact)
                     * (BUCKETS - exact)).astype(int)
    b = np.where(n < exact, n, np.minimum(large, BUCKETS - 1))
    return [int(np.argmax(b == i)) for i in range(BUCKETS)] + [SEQ]


def used_before_step(j):
    if j < HEADS - HG:
        return 3 + (3 * j) // HG
    return PROJ_UNITS + max(0, (j - (HEADS - HG)) // 2)


def split_plan():
    plan, done = [], 6
    for j in range(HEADS + 2):
        free = used_before_step(j) + SLOTS - (j < HEADS)
        plan.append(list(range(done, free)))
        done = max(done, free)
    return plan, done


def build(nc, x, rel_bias, w_qkv, w_o, ln_mix_g, ln_mix_b, w_up, w_down, ln_ffn_g, ln_ffn_b, out):
    F32, F32R = mybir.dt.float32, mybir.dt.float32r
    ACT = mybir.ActivationFunctionType
    ALU = mybir.AluOpType
    AX = mybir.AxisListType

    with ExitStack() as ctx:
        def sb(name, shape, dt=F32):
            return ctx.enter_context(nc.sbuf_tensor(name, shape, dt))

        def sem(name):
            return ctx.enter_context(nc.semaphore(name))

        w_raw = sb("w_raw", [P, SLOTS, UNIT])
        w_hi = sb("w_hi", [P, SLOTS, UNIT], F32R)
        w_lo = sb("w_lo", [P, SLOTS, UNIT], F32R)
        h = sb("h", [P, TT, D])
        xT_hi = sb("xT_hi", [P, KT, SEQ], F32R)
        xT_lo = sb("xT_lo", [P, KT, SEQ], F32R)
        xT32 = sb("xT32", [P, 2, SEQ])
        qkv_hi = sb("qkv_hi", [P, 2, 3, 512], F32R)
        qkv_lo = sb("qkv_lo", [P, 2, 3, 512], F32R)
        oT_hi = sb("oT_hi", [P, KT, SEQ], F32R)
        oT_lo = sb("oT_lo", [P, KT, SEQ], F32R)
        bias_rows = sb("bias_rows", [P, HEADS * SEQ])
        z = sb("z", [P, 2, SW])
        p = sb("p", [P, 2, SW])
        cum = sb("cum", [P, SW])
        pT_hi = sb("pT_hi", [P, 2, SW], F32R)
        pT_lo = sb("pT_lo", [P, 2, SW], F32R)
        relu = sb("relu", [P, 2, 512])
        u = sb("u", [P, 512])
        mask = sb("mask", [P, SW])
        ident = sb("ident", [P, P])
        relT = sb("relT", [HEADS, BUCKETS])
        by_dist = sb("by_dist", [HEADS, SW])
        gb_in = sb("gb_in", [8 * KT, P])
        gbT = sb("gbT", [P, 8 * KT])
        negmax = sb("negmax", [P, 2, 2])
        sums = sb("sums", [P, 2, 2])
        rinv = sb("rinv", [P, 2, 2])
        stats = sb("stats", [P, TT, 2, 6])
        mv = sb("mv", [P, TT, 2])
        veps = sb("veps", [P, TT])
        lnv = sb("lnv", [P, TT])
        rs0 = sb("rs0", [P, TT])
        nt = sb("nt", [P, TT, 2])
        rstd = sb("rstd", [P, TT])
        nmr = sb("nmr", [P, 1])
        ps = ctx.enter_context(nc.psum_tensor("ps", [P, 8, 512], F32))
        dist_dram = nc.dram_tensor("dist_dram", (HEADS, SW), F32, kind="Internal")

        bias = bias_rows[:, :].rearrange("p (h k) -> p h k", h=HEADS)
        gb_rows = bias_rows[:, :].rearrange("p (a d) -> p a d", a=4)

        raw_loaded = [sem(f"raw_loaded{s}") for s in range(SLOTS)]
        hi_done = sem("hi_done")
        lo_done = sem("lo_done")
        unit_used = sem("unit_used")
        x_loaded = [sem(f"x_loaded{t}") for t in range(TT)]
        gb_loaded = sem("gb_loaded")
        rel_loaded = sem("rel_loaded")
        dist_stored = sem("dist_stored")
        bias_loaded = sem("bias_loaded")
        rows_loaded = sem("rows_loaded")
        out_stored = sem("out_stored")
        const_ready = sem("const_ready")
        pool_own = sem("pool_own")
        dve_own = sem("dve_own")
        act_own = sem("act_own")
        gbT_psum = sem("gbT_psum")
        gbT_ready = sem("gbT_ready")
        xhat0_ready = sem("xhat0_ready")
        xhat1_ready = sem("xhat1_ready")
        xT_psum = sem("xT_psum")
        xT32_ready = sem("xT32_ready")
        xT_ready = sem("xT_ready")
        h_ready = sem("h_ready")
        var_ready = sem("var_ready")
        rs0_ready = sem("rs0_ready")
        rstd_ready = sem("rstd_ready")
        piece_loaded = [sem(f"piece_loaded{q}") for q in range(4)]
        piece_hi = sem("piece_hi")
        piece_lo = sem("piece_lo")
        qkv_hi_ready = sem("qkv_hi_ready")
        qkv_ready = sem("qkv_ready")
        score_done = sem("score_done")
        z_ready = sem("z_ready")
        logit_ready = sem("logit_ready")
        soft_done = sem("soft_done")
        exp_done = sem("exp_done")
        prob_ready = sem("prob_ready")
        pT_psum = sem("pT_psum")
        pT_hi_ready = sem("pT_hi_ready")
        pT_ready = sem("pT_ready")
        pv_done = sem("pv_done")
        oT_hi_ready = sem("oT_hi_ready")
        oT_ready = sem("oT_ready")
        relu_ready = sem("relu_ready")
        uT_ready = sem("uT_ready")
        acc_done = sem("acc_done")
        y_ready = sem("y_ready")

        def f32(ap):
            return ap.bitcast(F32)

        class Own:
            def __init__(self, s):
                self.s, self.n, self.shift = s, 0, 0

            def mark(self, ins):
                ins.then_inc(self.s, 1)
                self.n += 1

            def wait(self, eng):
                eng.wait_ge(self.s, self.n + self.shift)

        def uT(t, c):
            return t[:, c % 2, 0, :].rearrange("p (k s) -> p k s", k=FC // P)

        SPLITS, SPLIT_DONE = split_plan()
        assert SPLIT_DONE == ATT_UNITS + 2
        A_STEPS = HEADS + 2
        block = ctx.enter_context(nc.Block())

        @block.sync
        def _(sp):
            for t in range(TT):
                sp.dma_start(h[:, t, :], x[0, t * P:(t + 1) * P, :]).then_inc(x_loaded[t], 16)

            first = w_qkv[0].rearrange("(q k p) n -> q p k n", p=P, q=4)
            for q in range(4):
                sp.dma_start(w_raw[:, 0, q * 512:(q + 1) * 512].rearrange("p (k n) -> p k n", k=2),
                             first[q, :, :, 0:GC]).then_inc(piece_loaded[q], 16)

            def load(n, slot, src, shape, always=False):
                if always or n >= SLOTS:
                    sp.wait_ge(lo_done, n - SLOTS + 1)
                dst = w_raw[:, slot, :].rearrange("p (k n) -> p k n", k=shape)
                sp.dma_start(dst, src).then_inc(raw_loaded[slot], 16)

            for l in range(DEPTH):
                n0 = l * LAYER_UNITS
                qkv_l = w_qkv[l].rearrange("(k p) (w n) -> p k w n", p=P, w=3)
                o_l = w_o[l].rearrange("(g k p) n -> p g k n", p=P, g=GROUPS)
                up_l = w_up[l].rearrange("(k p) n -> p k n", p=P)
                down_l = w_down[l].rearrange("(k p) n -> p k n", p=P)
                for m in range(1 if l == 0 else 0, PROJ_UNITS):
                    g, w = divmod(m, 3)
                    load(n0 + m, m % SLOTS, qkv_l[:, :, w, g * GC:(g + 1) * GC], KT)
                for g in range(GROUPS):
                    m = PROJ_UNITS + g
                    load(n0 + m, m % SLOTS, o_l[:, g], GC // P)

                def load_up(n, slot, c):
                    load(n, slot, up_l[:, :, bass.ds(c * FC, FC)], KT, True)

                def load_down(n, slot, c):
                    load(n, slot, down_l[:, bass.ds(c * (FC // P), FC // P), :], FC // P, True)

                f0 = n0 + ATT_UNITS
                load_up(f0, 0, 0)
                with sp.Fori(0, TRIPS) as i:
                    load_up(f0 + 1 + 4 * i, 1, 2 * i + 1)
                    load_down(f0 + 2 + 4 * i, 2, 2 * i)
                    load_up(f0 + 3 + 4 * i, 3, 2 * i + 2)
                    load_down(f0 + 4 + 4 * i, 0, 2 * i + 1)
                load_up(f0 + 29, 1, CHUNKS - 1)
                load_down(f0 + 30, 2, CHUNKS - 2)
                load_down(f0 + 31, 3, CHUNKS - 1)

            for q in range(2 * TT):
                t, s = divmod(q, 2)
                half = slice(s * 512, (s + 1) * 512)
                sp.wait_ge(y_ready, q + 1)
                sp.dma_start(out[0, t * P:(t + 1) * P, half], h[:, t, half]).then_inc(out_stored, 16)
            sp.wait_ge(out_stored, 16 * 2 * TT)

        @block.gpsimd
        def _(pool):
            own = Own(pool_own)
            own.mark(pool.memset(ident[:, :], 0.0))
            own.mark(pool.memset(mask[:, :], 0.0))
            own.mark(pool.memset(by_dist[:, :], -BIG))
            pool.dma_start(relT[:, :], rel_bias.rearrange("b h -> h b"),
                           allow_slow_non_contiguous=True).then_inc(rel_loaded, 16)
            own.wait(pool)
            pool.affine_select(out=ident[:, :], in_=ident[:, :], compare_op=ALU.not_equal, fill=1.0,
                               base=0, pattern=[[-1, P]], channel_multiplier=1).then_inc(const_ready, 1)
            diag = mask[:, P:SW].rearrange("p (a k) -> p a k", a=2)
            pool.affine_select(out=diag, in_=diag, compare_op=ALU.is_gt, fill=-BIG,
                               base=0, pattern=[[0, 2], [-1, P]], channel_multiplier=1).then_inc(const_ready, 1)
            pool.wait_ge(rel_loaded, 16)
            starts = bucket_starts()
            exact = BUCKETS // 2
            own.mark(pool.tensor_copy(by_dist[:, P - 1:P - 1 + exact], relT[:, 0:exact]))
            for b in range(exact, BUCKETS):
                lo, hi = starts[b], starts[b + 1]
                own.mark(pool.tensor_copy(by_dist[:, P - 1 + lo:P - 1 + hi],
                                          relT[:, b:b + 1].to_broadcast([HEADS, hi - lo])))
            own.wait(pool)
            pool.dma_start(dist_dram.ap(), by_dist[:, :]).then_inc(dist_stored, 16)
            pool.wait_ge(dist_stored, 16)
            pool.dma_start(bias, bass.AP(dist_dram, 0, [[1, P], [SW, HEADS], [1, SEQ]])).then_inc(bias_loaded, 16)

            for l in range(DEPTH):
                if l == 0:
                    pool.wait_ge(z_ready, HEADS)
                else:
                    pool.wait_ge(h_ready, 2 * TT)
                for a, v in enumerate((ln_mix_g, ln_mix_b, ln_ffn_g, ln_ffn_b)):
                    pool.dma_start(gb_rows[:, a, :], bass.AP(v.tensor, l * D, [[0, P], [1, D]])).then_inc(rows_loaded, 16)
                pool.wait_ge(rows_loaded, 64 * (l + 1))
                for s in range(2):
                    ln = 2 * l + s + 1
                    if ln == 2 * DEPTH:
                        break
                    pool.wait_ge(xT_psum, 4 * (ln + 1))
                    for t in range(TT):
                        own.mark(pool.tensor_tensor(h[:, t, :], h[:, t, :], gb_rows[:, 2 * s, :], ALU.mult))
                        own.wait(pool)
                        pool.tensor_tensor(h[:, t, :], h[:, t, :], gb_rows[:, 2 * s + 1, :],
                                           ALU.add).then_inc(h_ready, 1)

        @block.scalar
        def _(act):
            own = Own(act_own)
            act.preload_act_table_set("natural_log_exp_and_others")
            for a, v in enumerate((ln_mix_g, ln_mix_b, ln_ffn_g, ln_ffn_b)):
                act.dma_start(gb_in[a * 2 * KT:(a + 1) * 2 * KT, :],
                              v.rearrange("l (k p) -> (l k) p", p=P)).then_inc(gb_loaded, 16)

            def split_hi(n, slot, always=False, uses=None):
                act.wait_ge(raw_loaded[slot], uses if uses is not None else 16 * (n // SLOTS + (slot > 0)))
                if always or n >= SLOTS:
                    act.wait_ge(unit_used, n - SLOTS + 1)
                act.copy(w_hi[:, slot, :], w_raw[:, slot, :]).then_inc(hi_done, 1)

            def split_piece(q):
                act.wait_ge(piece_loaded[q], 16)
                part = slice(q * 512, (q + 1) * 512)
                act.copy(w_hi[:, 0, part], w_raw[:, 0, part]).then_inc(piece_hi, 1)

            def xT_evac(ln):
                for k in range(KT):
                    if k % 2 == 0:
                        act.wait_ge(xT_psum, 4 * ln + k // 2 + 1)
                    if k >= 2 or ln >= 1:
                        act.wait_ge(xT_ready, 8 * ln + k - 1)
                    src = ps[:, XT + k // 2, (k % 2) * SEQ:(k % 2 + 1) * SEQ]
                    if ln == 0:
                        act.copy(xT32[:, k % 2, :], src).then_inc(xT32_ready, 1)
                        if k % 2 == 1:
                            split_piece(k // 2)
                    else:
                        if ln == 1 and k == 0:
                            act.wait_ge(gbT_ready, 1)
                        l, s = divmod(ln - 1, 2)
                        col = 4 * s * KT + l * KT + k
                        gain, offs = gbT[:, col:col + 1], gbT[:, col + 2 * KT:col + 2 * KT + 1]
                        act.activation(xT32[:, k % 2, :], src, ACT.Identity, bias=offs,
                                       scale=gain).then_inc(xT32_ready, 1)

            def ln_rstd(ln):
                for t in range(TT):
                    act.wait_ge(var_ready, TT * (ln - 1) + t + 1)
                    own.mark(act.activation(lnv[:, t:t + 1], veps[:, t:t + 1], ACT.Ln))
                    own.wait(act)
                    act.activation(rs0[:, t:t + 1], lnv[:, t:t + 1], ACT.Exp, scale=-0.5).then_inc(rs0_ready, 1)
                    if t == 0 and ln < 2 * DEPTH:
                        act.wait_ge(rstd_ready, ln)
                        act.activation(h[:, 0, :], h[:, 0, :], ACT.Identity, bias=nmr[:, :],
                                       scale=rstd[:, 0:1]).then_inc(xhat0_ready, 1)

            def qkv_evac(l, g, w):
                m = 3 * g + w
                act.wait_ge(unit_used, LAYER_UNITS * l + m + 1)
                if g >= 2:
                    act.wait_ge(pv_done, HEADS * l + HG * (g - 1))
                act.activation(qkv_hi[:, g % 2, w, :], ps[:, PROJ + m % 2, :], ACT.Copy,
                               scale=QK_SCALE if w == 0 else 1.0).then_inc(qkv_hi_ready, 1)

            def exp_part(l, j):
                hd = HEADS * l + j
                zj, pj = z[:, j % 2, :], p[:, j % 2, :]
                act.wait_ge(logit_ready, hd + 1)
                if l == 0:
                    if j >= 2:
                        act.wait_ge(pT_psum, hd - 1)
                    act.activation(pj[:, ROWS1], zj[:, ROWS1], ACT.Exp, bias=negmax[:, j % 2, 0:1],
                                   accum_out=sums[:, j % 2, 0:1])
                    act.activation(pj[:, ROWS0], zj[:, ROWS0], ACT.Exp, bias=negmax[:, j % 2, 1:2],
                                   accum_out=sums[:, j % 2, 1:2]).then_inc(exp_done, 1)
                else:
                    act.activation(pj, zj, ACT.Exp).then_inc(exp_done, 1)

            def softplus_part(l, j):
                hd = HEADS * l + j
                zj, pj = z[:, j % 2, :], p[:, j % 2, :]
                act.wait_ge(z_ready, hd + 1)
                act.wait_ge(pT_psum, hd - 1)
                if j >= 2:
                    act.wait_ge(logit_ready, hd - 1)
                act.activation(relu[:, j % 2, 0:SW], zj, ACT.Relu)
                own.mark(act.activation(pj, zj, ACT.Abs))
                own.wait(act)
                own.mark(act.activation(pj, pj, ACT.Exp, scale=-1.0))
                own.wait(act)
                act.activation(pj, pj, ACT.Ln, bias=1.0).then_inc(soft_done, 1)

            def pT_evac(l, j):
                hd = HEADS * l + j
                act.wait_ge(pT_psum, hd + 1)
                if j >= 2:
                    act.wait_ge(pv_done, hd - 1)
                act.copy(pT_hi[:, j % 2, :], ps[:, PT, 0:SW]).then_inc(pT_hi_ready, 1)

            def o_evac(l, j):
                hd = HEADS * l + j
                rows = slice(DH * (j % 2), DH * (j % 2) + DH)
                act.wait_ge(pv_done, hd + 1)
                act.copy(oT_hi[rows, j // 2, :], ps[rows, OUT, 0:SEQ]).then_inc(oT_hi_ready, 1)

            def relu_evac(k, l, c, first=False):
                act.wait_ge(unit_used, LAYER_UNITS * l + ATT_UNITS + (1 if first else 2 * c))
                if not first:
                    act.wait_ge(uT_ready, CHUNKS * l + c)
                act.activation(relu[:, k, :], ps[:, UP0 if first else UP + k, :], ACT.Relu).then_inc(relu_ready, 1)

            xT_evac(0)
            for n in range(1, SLOTS):
                split_hi(n, n)
            for l in range(DEPTH):
                n0 = l * LAYER_UNITS
                qkv_evac(l, 0, 0)
                split_hi(n0 + 4, 0)
                qkv_evac(l, 0, 1)
                split_hi(n0 + 5, 1)
                qkv_evac(l, 0, 2)
                evac = 3
                for j in range(A_STEPS):
                    if l == 1 and j >= 2:
                        pT_evac(l, j - 2)
                    for m in SPLITS[j]:
                        split_hi(n0 + m, m % SLOTS)
                    if l == 0:
                        if j < HEADS:
                            exp_part(l, j)
                        if 1 <= j <= HEADS:
                            pT_evac(l, j - 1)
                    else:
                        if 1 <= j <= HEADS:
                            exp_part(l, j - 1)
                        if j < HEADS:
                            softplus_part(l, j)
                    while evac < min(PROJ_UNITS, used_before_step(j + 1)):
                        qkv_evac(l, evac // 3, evac % 3)
                        evac += 1
                    if 2 <= j:
                        o_evac(l, j - 2)
                ln_rstd(2 * l + 1)
                xT_evac(2 * l + 1)
                for m in range(SPLIT_DONE, ATT_UNITS + 3):
                    split_hi(n0 + m, m % SLOTS)

                f0 = n0 + ATT_UNITS
                relu_evac(0, l, 0, first=True)
                r0 = 16 * (f0 // SLOTS)
                with act.Fori(0, TRIPS) as i:
                    split_hi(f0 + 3 + 4 * i, 3, True, r0 + 16 + 16 * i)
                    split_hi(f0 + 4 + 4 * i, 0, True, r0 + 16 + 16 * i)
                    relu_evac(1, l, 2 * i + 1)
                    split_hi(f0 + 5 + 4 * i, 1, True, r0 + 32 + 16 * i)
                    split_hi(f0 + 6 + 4 * i, 2, True, r0 + 32 + 16 * i)
                    relu_evac(0, l, 2 * i + 2)
                split_hi(f0 + 31, 3)
                if l + 1 < DEPTH:
                    split_hi(f0 + 32, 0)
                relu_evac(1, l, CHUNKS - 1)
                if l + 1 < DEPTH:
                    split_hi(f0 + 33, 1)
                ln_rstd(2 * l + 2)
                if l + 1 < DEPTH:
                    xT_evac(2 * l + 2)
                    split_hi(f0 + 34, 2)
                    split_hi(f0 + 35, 3)

        @block.vector
        def _(dve):
            own = Own(dve_own)

            def split_lo(n, slot):
                dve.wait_ge(hi_done, n)
                dve.tensor_tensor(w_lo[:, slot, :], w_raw[:, slot, :], f32(w_hi[:, slot, :]),
                                  ALU.subtract).then_inc(lo_done, 1)

            def split_piece(q):
                dve.wait_ge(piece_hi, q + 1)
                part = slice(q * 512, (q + 1) * 512)
                dve.tensor_tensor(w_lo[:, 0, part], w_raw[:, 0, part], f32(w_hi[:, 0, part]),
                                  ALU.subtract).then_inc(piece_lo if q < 3 else lo_done, 1)

            def xT_evac(ln):
                for k in range(KT):
                    dve.wait_ge(xT32_ready, 8 * ln + k + 1)
                    own.mark(dve.tensor_copy(xT_hi[:, k, :], xT32[:, k % 2, :]))
                    own.wait(dve)
                    dve.tensor_tensor(xT_lo[:, k, :], xT32[:, k % 2, :], f32(xT_hi[:, k, :]),
                                      ALU.subtract).then_inc(xT_ready, 1)
                    if ln == 0 and k % 2 == 1:
                        split_piece(k // 2)

            def norm(ln):
                def add_and_measure(t, s):
                    hs = h[:, t, s * 512:(s + 1) * 512]
                    if t == 0 and s == 0 and ln >= 2:
                        dve.wait_ge(h_ready, TT * (ln - 1))
                    if 2 * t + s < 3:
                        dve.wait_ge(acc_done, 3 * (ln - 1) + 2 * t + s + 1)
                    else:
                        l, ffn = divmod(ln - 1, 2)
                        dve.wait_ge(unit_used, LAYER_UNITS * l + (LAYER_UNITS if ffn else ATT_UNITS))
                    own.mark(dve.scalar_tensor_tensor(hs, hs, ALPHA, ps[:, ACC + 2 * t + s, :],
                                                      ALU.mult, ALU.add))
                    own.wait(dve)
                    own.mark(dve.bn_stats(stats[:, t, s, :], hs))

                def variance(t):
                    own.wait(dve)
                    own.mark(dve.bn_aggr(mv[:, t, :], stats[:, t, :, :]))
                    own.wait(dve)
                    dve.tensor_scalar(veps[:, t:t + 1], mv[:, t, 1:2], EPS, None,
                                      ALU.add).then_inc(var_ready, 1)

                def centre_and_scale(t):
                    dve.wait_ge(rs0_ready, TT * (ln - 1) + t + 1)
                    r0, v = rs0[:, t:t + 1], veps[:, t:t + 1]
                    own.mark(dve.scalar_tensor_tensor(nt[:, t, 0:1], r0, v, r0, ALU.mult, ALU.mult))
                    own.wait(dve)
                    own.mark(dve.tensor_scalar(nt[:, t, 1:2], nt[:, t, 0:1], -0.5, 1.5, ALU.mult, ALU.add))
                    own.wait(dve)
                    own.mark(dve.tensor_tensor(rstd[:, t:t + 1], r0, nt[:, t, 1:2], ALU.mult))
                    own.wait(dve)
                    if ln == 2 * DEPTH:
                        for s in range(2):
                            half = slice(s * 512, (s + 1) * 512)
                            dve.scalar_tensor_tensor(h[:, t, half], h[:, t, half], rstd[:, t:t + 1],
                                                     gb_rows[:, 3, half], ALU.mult, ALU.add).then_inc(y_ready, 1)
                    elif t == 0:
                        dve.scalar_tensor_tensor(nmr[:, :], mv[:, 0, 0:1], -1.0, rstd[:, 0:1],
                                                 ALU.mult, ALU.mult).then_inc(rstd_ready, 1)
                    else:
                        for s in range(2):
                            half = slice(s * 512, (s + 1) * 512)
                            dve.tensor_scalar(h[:, 1, half], h[:, 1, half], mv[:, 1, 0:1], rstd[:, 1:2],
                                              ALU.subtract, ALU.mult).then_inc(xhat1_ready, 1)

                def centre_with_gain(t):
                    if ln == 2 * DEPTH:
                        for s in range(2):
                            half = slice(s * 512, (s + 1) * 512)
                            own.mark(dve.scalar_tensor_tensor(h[:, t, half], h[:, t, half], mv[:, t, 0:1],
                                                              gb_rows[:, 2, half], ALU.subtract, ALU.mult))

                if ln == 2 * DEPTH:
                    dve.wait_ge(rows_loaded, 64 * DEPTH)
                add_and_measure(0, 0)
                add_and_measure(0, 1)
                variance(0)
                centre_with_gain(0)
                add_and_measure(1, 0)
                centre_and_scale(0)
                add_and_measure(1, 1)
                variance(1)
                centre_with_gain(1)
                centre_and_scale(1)

            def qkv_evac(l, g, w):
                m = 3 * g + w
                dve.wait_ge(qkv_hi_ready, PROJ_UNITS * l + m + 1)
                dve.scalar_tensor_tensor(qkv_lo[:, g % 2, w, :], ps[:, PROJ + m % 2, :],
                                         QK_SCALE if w == 0 else 1.0, f32(qkv_hi[:, g % 2, w, :]),
                                         ALU.mult, ALU.subtract).then_inc(qkv_ready, 1)

            def scores(l, j):
                hd = HEADS * l + j
                s, zj = ps[:, SCORE + j % 2, 0:SW], z[:, j % 2, :]
                dve.wait_ge(score_done, hd + 1)
                if hd >= 2:
                    dve.wait_ge(exp_done, hd - 1)
                if l == 0:
                    if j == 0:
                        dve.wait_ge(bias_loaded, 16)
                    rev = bass.AP(bias_rows, j * SEQ + SEQ - 1, [[HEADS * SEQ, P], [-1, SEQ]])
                    rev0 = bass.AP(bias_rows, j * SEQ + P - 1, [[HEADS * SEQ, P], [-1, P]])
                    own.mark(dve.scalar_tensor_tensor(zj[:, ROWS1], s[:, ROWS1], 1.0, rev, ALU.mult, ALU.add))
                    dve.scalar_tensor_tensor(zj[:, ROWS0], s[:, ROWS0], 1.0, rev0, ALU.mult,
                                             ALU.add).then_inc(z_ready, 1)
                    own.wait(dve)
                    dve.reduce_max(negmax[:, j % 2, 0:1], zj[:, ROWS1], AX.X, negate=True)
                    dve.wait_ge(z_ready, hd + 1)
                    dve.reduce_max(negmax[:, j % 2, 1:2], zj[:, ROWS0], AX.X, negate=True).then_inc(logit_ready, 1)
                else:
                    if j == 0:
                        dve.wait_ge(const_ready, 2)
                    dve.scalar_tensor_tensor(zj, s, 1.0, mask[:, :], ALU.mult, ALU.add).then_inc(z_ready, 1)

            def normalise(l, j):
                hd = HEADS * l + j
                dve.wait_ge(exp_done, hd + 1)
                own.mark(dve.reciprocal(rinv[:, j % 2, :], sums[:, j % 2, :]))
                own.wait(dve)
                for i, rows in enumerate((ROWS1, ROWS0)):
                    pj = p[:, j % 2, rows]
                    dve.tensor_scalar(pj, pj, rinv[:, j % 2, i:i + 1], None, ALU.mult).then_inc(prob_ready, 1)

            def stick(l, j):
                hd = HEADS * l + j
                zj, pj = z[:, j % 2, :], p[:, j % 2, :]
                dve.wait_ge(soft_done, j + 1)
                for rows in (ROWS1, ROWS0):
                    n = rows.stop - rows.start
                    back = bass.AP(p, (j % 2) * SW + rows.stop - 1, [[2 * SW, P], [-1, n]])
                    back_relu = bass.AP(relu, (j % 2) * 512 + rows.stop - 1, [[2 * 512, P], [-1, n]])
                    back_sum = bass.AP(cum, rows.stop - 1, [[SW, P], [-1, n]])
                    own.mark(dve.tensor_tensor_scan(back_sum, back_relu, back, 0.0, ALU.add, ALU.add))
                own.wait(dve)
                dve.tensor_tensor(zj, zj, cum[:, :], ALU.subtract).then_inc(logit_ready, 1)

            def pT_evac(l, j):
                hd = HEADS * l + j
                dve.wait_ge(pT_hi_ready, hd + 1)
                dve.tensor_tensor(pT_lo[:, j % 2, :], ps[:, PT, 0:SW], f32(pT_hi[:, j % 2, :]),
                                  ALU.subtract).then_inc(pT_ready, 1)

            def o_evac(l, j):
                hd = HEADS * l + j
                rows = slice(DH * (j % 2), DH * (j % 2) + DH)
                dve.wait_ge(oT_hi_ready, hd + 1)
                dve.tensor_tensor(oT_lo[rows, j // 2, :], ps[rows, OUT, 0:SEQ], f32(oT_hi[rows, j // 2, :]),
                                  ALU.subtract).then_inc(oT_ready, 1)

            def square(k, l, c):
                dve.wait_ge(relu_ready, CHUNKS * l + c + 1)
                own.mark(dve.tensor_tensor(u[:, :], relu[:, k, :], relu[:, k, :], ALU.mult))
                own.wait(dve)
                own.mark(dve.tensor_copy(qkv_hi[:, k, 0, :], u[:, :]))
                own.wait(dve)
                dve.tensor_tensor(qkv_lo[:, k, 0, :], u[:, :], f32(qkv_hi[:, k, 0, :]),
                                  ALU.subtract).then_inc(uT_ready, 1)

            xT_evac(0)
            for n in range(1, SLOTS):
                split_lo(n, n)
            dve.wait_ge(gbT_psum, 1)
            dve.tensor_copy(gbT[:, :], ps[:, OUT, 0:8 * KT]).then_inc(gbT_ready, 1)
            for l in range(DEPTH):
                n0 = l * LAYER_UNITS
                qkv_evac(l, 0, 0)
                split_lo(n0 + 4, 0)
                qkv_evac(l, 0, 1)
                split_lo(n0 + 5, 1)
                qkv_evac(l, 0, 2)
                evac = 3
                for j in range(A_STEPS):
                    if l == 1:
                        if 1 <= j <= HEADS:
                            stick(l, j - 1)
                        if j >= 2:
                            pT_evac(l, j - 2)
                    if j < HEADS:
                        scores(l, j)
                    for m in SPLITS[j]:
                        split_lo(n0 + m, m % SLOTS)
                    if l == 0:
                        if 1 <= j <= HEADS:
                            pT_evac(l, j - 1)
                        if j < HEADS:
                            normalise(l, j)
                    while evac < min(PROJ_UNITS, used_before_step(j + 1)):
                        qkv_evac(l, evac // 3, evac % 3)
                        evac += 1
                    if 2 <= j:
                        o_evac(l, j - 2)
                norm(2 * l + 1)
                xT_evac(2 * l + 1)
                for m in range(SPLIT_DONE, ATT_UNITS + 3):
                    split_lo(n0 + m, m % SLOTS)

                f0 = n0 + ATT_UNITS
                square(0, l, 0)
                per_trip, start = 4, own.n
                with dve.Fori(0, TRIPS) as i:
                    own.shift = per_trip * i
                    split_lo(f0 + 3 + 4 * i, 3)
                    split_lo(f0 + 4 + 4 * i, 0)
                    square(1, l, 2 * i + 1)
                    split_lo(f0 + 5 + 4 * i, 1)
                    split_lo(f0 + 6 + 4 * i, 2)
                    square(0, l, 2 * i + 2)
                assert own.n == start + per_trip
                own.n, own.shift = start + per_trip * TRIPS, 0
                split_lo(f0 + 31, 3)
                if l + 1 < DEPTH:
                    split_lo(f0 + 32, 0)
                square(1, l, CHUNKS - 1)
                if l + 1 < DEPTH:
                    split_lo(f0 + 33, 1)
                norm(2 * l + 2)
                if l + 1 < DEPTH:
                    xT_evac(2 * l + 2)
                    split_lo(f0 + 34, 2)
                    split_lo(f0 + 35, 3)

        @block.tensor
        def _(pe):
            PASSES = ((0, 0), (0, 1), (1, 0))
            xT, w, qkv, oT, pT = (xT_hi, xT_lo), (w_hi, w_lo), (qkv_hi, qkv_lo), (oT_hi, oT_lo), (pT_hi, pT_lo)

            def transposes(ln):
                for t in range(TT):
                    for k in range(KT):
                        if ln == 0 and k == 0:
                            pe.wait_ge(x_loaded[t], 16)
                        if ln >= 1 and t == 0 and k == 0:
                            pe.wait_ge(xhat0_ready, ln)
                        if ln >= 1 and t == 1 and k % 4 == 0:
                            pe.wait_ge(xhat1_ready, 2 * (ln - 1) + k // 4 + 1)
                        o = (k % 2) * SEQ + t * P
                        mm = pe.transpose(ps[:, XT + k // 2, o:o + P], h[:, t, k * P:(k + 1) * P], ident[:, :])
                        if t == TT - 1 and k % 2 == 1:
                            mm.then_inc(xT_psum, 1)

            def feature_major(slot, bank, k, ln):
                wk = [t[:, slot, :].rearrange("p (k n) -> p k n", k=KT) for t in w]
                if ln is not None:
                    pe.wait_ge(xT_ready, 8 * ln + k + 1)
                for c in range(2):
                    for i, (a, b) in enumerate(PASSES):
                        mm = pe.matmul(ps[:, bank, c * SEQ:(c + 1) * SEQ], wk[a][:, k, c * P:(c + 1) * P],
                                       xT[b][:, k, :], start=(k == 0 and c == 0 and i == 0),
                                       stop=(k == KT - 1 and i == 2), skip_group_check=True)
                return mm

            def token_major(slot, bank, k):
                wk = [t[:, slot, :].rearrange("p (k n) -> p k n", k=KT) for t in w]
                for t in range(TT):
                    for i, (a, b) in enumerate(PASSES):
                        mm = pe.matmul(ps[:, bank, t * GC:(t + 1) * GC], xT[a][:, k, t * P:(t + 1) * P],
                                       wk[b][:, k, :], start=(k == 0 and t == 0 and i == 0),
                                       stop=(k == KT - 1 and i == 2), skip_group_check=True)
                return mm

            def proj(l, m, k):
                g, which = divmod(m, 3)
                n = l * LAYER_UNITS + m
                if n == 0 and k % 2 == 0 and k < KT - 2:
                    pe.wait_ge(piece_lo, k // 2 + 1)
                if (n > 0 and k == 0) or (n == 0 and k == KT - 2):
                    pe.wait_ge(lo_done, n + 1)
                if k == 0:
                    if m >= 2:
                        pe.wait_ge(qkv_ready, PROJ_UNITS * l + m - 1)
                if which < 2:
                    mm = feature_major(m % SLOTS, PROJ + m % 2, k, 2 * l if m == 0 else None)
                else:
                    mm = token_major(m % SLOTS, PROJ + m % 2, k)
                if k == KT - 1:
                    mm.then_inc(unit_used, 1)

            def sum_part(slot, src, k_src, k, t, first, last, halves=(0, 1)):
                wk = [x[:, slot, :].rearrange("p (k n) -> p k n", k=FC // P) for x in w]
                for s in halves:
                    for i, (a, b) in enumerate(PASSES):
                        mm = pe.matmul(ps[:, ACC + 2 * t + s, :], src[a][:, k_src, t * P:(t + 1) * P],
                                       wk[b][:, k, s * 512:(s + 1) * 512],
                                       start=(first and i == 0), stop=(last and i == 2))
                return mm

            def o_slice(l, q):
                g, r = divmod(q, 4)
                k, t = divmod(r, 2)
                n = l * LAYER_UNITS + PROJ_UNITS + g
                if r == 0:
                    pe.wait_ge(lo_done, n + 1)
                    pe.wait_ge(oT_ready, HEADS * l + HG * (g + 1))
                if q == 1:
                    pe.wait_ge(qkv_ready, PROJ_UNITS * (l + 1))
                mm = sum_part((PROJ_UNITS + g) % SLOTS, oT, 2 * g + k, k, t, q < 2, False)
                if r == 3:
                    mm.then_inc(unit_used, 1)

            def last_units(units):
                for slot, src, k0, waits in units:
                    for which, count in waits:
                        pe.wait_ge(which, count)
                    final = slot == units[-1][0]
                    for s in range(2):
                        for k in range(2):
                            mm = sum_part(slot, src, k0 + k, k, 0, False, final and k == 1, halves=(s,))
                        if final:
                            mm.then_inc(acc_done, 1)
                for s in range(2):
                    for slot, src, k0, _ in units:
                        final = slot == units[-1][0]
                        for k in range(2):
                            mm = sum_part(slot, src, k0 + k, k, 1, False, final and k == 1, halves=(s,))
                        if s == 1:
                            mm.then_inc(unit_used, 1)
                    if s == 0:
                        mm.then_inc(acc_done, 1)

            def attend_scores(l, j):
                hd = HEADS * l + j
                par, tile, r0 = (j // HG) % 2, (j % HG) // 2, DH * (j % 2)
                if j % HG == 0:
                    pe.wait_ge(qkv_ready, PROJ_UNITS * l + 3 * (j // HG) + 2)
                if j >= 2:
                    pe.wait_ge(z_ready, hd - 1)
                q = [t[r0:r0 + DH, par, 0, tile * SEQ:(tile + 1) * SEQ] for t in qkv]
                kk = [t[r0:r0 + DH, par, 1, tile * SEQ:(tile + 1) * SEQ] for t in qkv]
                for cols, t, nk in ((ROWS1, 1, SEQ), (ROWS0, 0, P)):
                    for i, (a, b) in enumerate(PASSES):
                        mm = pe.matmul(ps[:, SCORE + j % 2, cols], q[a][:, t * P:(t + 1) * P], kk[b][:, 0:nk],
                                       start=(i == 0), stop=(i == 2))
                mm.then_inc(score_done, 1)

            def attend_transpose(l, j):
                hd = HEADS * l + j
                if l == 0:
                    pe.wait_ge(prob_ready, 2 * (j + 1))
                else:
                    pe.wait_ge(exp_done, hd + 1)
                if hd >= 1:
                    pe.wait_ge(pT_ready, hd)
                pj = p[:, j % 2, :]
                for dst, src in ((0, 256), (128, 0), (256, 128)):
                    mm = pe.transpose(ps[:, PT, dst:dst + P], pj[:, src:src + P], ident[:, :])
                mm.then_inc(pT_psum, 1)

            def attend_values(l, j):
                hd = HEADS * l + j
                par, pair = (j // HG) % 2, (j % HG) // 2
                pe.wait_ge(pT_ready, hd + 1)
                if j % HG == 0:
                    pe.wait_ge(qkv_ready, PROJ_UNITS * l + 3 * (j // HG) + 3)
                if hd >= 1:
                    pe.wait_ge(oT_ready, hd)
                for kt, dst, src in ((0, slice(0, SEQ), slice(0, SEQ)), (1, slice(P, SEQ), slice(SEQ, SW))):
                    for i, (a, b) in enumerate(PASSES):
                        v = qkv[a][:, par, 2, kt * GC + pair * P:kt * GC + (pair + 1) * P]
                        mm = pe.matmul(ps[:, OUT, dst], v, pT[b][:, j % 2, src],
                                       start=(kt == 0 and i == 0), stop=(kt == 1 and i == 2))
                mm.then_inc(pv_done, 1)

            def up(l, c, n, slot, bank, ln=None, wait_bank=True):
                pe.wait_ge(lo_done, n + 1)
                if wait_bank:
                    pe.wait_ge(relu_ready, CHUNKS * l + c - 1)
                for k in range(KT):
                    mm = feature_major(slot, bank, k, ln)
                mm.then_inc(unit_used, 1)

            def down(l, c, n, slot, par, first=False):
                pe.wait_ge(lo_done, n + 1)
                pe.wait_ge(uT_ready, CHUNKS * l + c + 1)
                src = [uT(t, par) for t in qkv]
                for k in range(2):
                    for t in range(TT):
                        mm = sum_part(slot, src, k, k, t, first and k == 0, False)
                mm.then_inc(unit_used, 1)

            pe.wait_ge(const_ready, 2)
            for l in range(DEPTH):
                transposes(2 * l)
                for m in range(3):
                    for k in range(KT):
                        proj(l, m, k)
                    if l == 0 and m == 0:
                        pe.wait_ge(gb_loaded, 64)
                        pe.transpose(ps[:, OUT, 0:8 * KT], gb_in[:, :],
                                     ident[0:8 * KT, 0:8 * KT]).then_inc(gbT_psum, 1)
                ksteps = iter([(m, k) for m in range(3, PROJ_UNITS) for k in range(KT)])
                slices = iter(range(4 * (GROUPS - 1)))
                for j in range(A_STEPS):
                    def fill():
                        if j < HEADS - HG:
                            for _ in range(2):
                                proj(l, *next(ksteps))
                        else:
                            q = next(slices, None)
                            if q is not None:
                                o_slice(l, q)
                    if l == 1 and j >= 2:
                        attend_transpose(l, j - 2)
                    fill()
                    if j < HEADS:
                        attend_scores(l, j)
                    fill()
                    if l == 0 and 1 <= j <= HEADS:
                        attend_transpose(l, j - 1)
                    if j < HEADS - HG:
                        fill()
                    if j >= 2:
                        attend_values(l, j - 2)
                n = l * LAYER_UNITS + ATT_UNITS - 1
                last_units([((ATT_UNITS - 1) % SLOTS, oT, KT - 2,
                             [(lo_done, n + 1), (oT_ready, HEADS * (l + 1))])])

                transposes(2 * l + 1)
                f0 = l * LAYER_UNITS + ATT_UNITS
                up(l, 0, f0, 0, UP0, ln=2 * l + 1, wait_bank=False)
                up(l, 1, f0 + 1, 1, UP + 1, wait_bank=False)
                down(l, 0, f0 + 2, 2, 0, first=True)
                up(l, 2, f0 + 3, 3, UP)
                down(l, 1, f0 + 4, 0, 1)
                with pe.Fori(1, TRIPS) as i:
                    up(l, 2 * i + 1, f0 + 1 + 4 * i, 1, UP + 1)
                    down(l, 2 * i, f0 + 2 + 4 * i, 2, 0)
                    up(l, 2 * i + 2, f0 + 3 + 4 * i, 3, UP)
                    down(l, 2 * i + 1, f0 + 4 + 4 * i, 0, 1)
                up(l, CHUNKS - 1, f0 + 29, 1, UP + 1)
                last_units([(2, [uT(t, 0) for t in qkv], 0,
                             [(lo_done, f0 + 31), (uT_ready, CHUNKS * (l + 1) - 1)]),
                            (3, [uT(t, 1) for t in qkv], 0,
                             [(lo_done, f0 + 32), (uT_ready, CHUNKS * (l + 1))])])


INS = ["x", "rel_bias", "w_qkv", "w_o", "ln_mix_g", "ln_mix_b", "w_up", "w_down", "ln_ffn_g", "ln_ffn_b"]


def kernel(**inputs):
    import numpy as _np
    import concourse.bacc as _bacc
    from concourse import mybir as _mybir
    from concourse.bass_utils import run_bass_kernel_spmd as _run

    nc = _bacc.Bacc("TRN2", target_bir_lowering=False, num_devices=1)
    arrays, args = {}, []
    for name in INS:
        a = _np.ascontiguousarray(inputs[name])
        arrays[f"in_{name}_dram"] = a
        args.append(nc.dram_tensor(f"in_{name}_dram", a.shape, _mybir.dt.from_np(a.dtype), kind="ExternalInput").ap())
    args.append(nc.dram_tensor("out_0_dram", (1, SEQ, D), _mybir.dt.float32, kind="ExternalOutput").ap())
    build(nc, *args)
    r = _run(nc, [arrays], core_ids=[0])
    return r.results[0]["out_0_dram"]
```

```python
import math
from contextlib import ExitStack

import numpy as np
import concourse.bass as bass
from concourse import mybir

D = 1024
SEQ = 256
DEPTH = 2
HEADS = 16
DH = D // HEADS
FF = 4 * D
BUCKETS = 32
MAX_DIST = 128
EPS = 1e-5
ALPHA = (2.0 * DEPTH) ** 0.25
QK_SCALE = DH ** -0.5
HALVES = [slice(c, c + 512) for c in (0, 512)]
XHAT1_PARTS = [slice(0, 256), slice(256, 512), slice(512, D)]
ACC_PARTS = 3
BIG = 1.0e30

P = 128
TT = SEQ // P
KT = D // P
HG = 4
GROUPS = HEADS // HG
GC = HG * DH
FC = 256
CHUNKS = FF // FC
SLOTS = 4
UNIT = KT * GC
PROJ_UNITS = 3 * GROUPS
ATT_UNITS = PROJ_UNITS + GROUPS
LAYER_UNITS = ATT_UNITS + 2 * CHUNKS
POOL_FIRST = ATT_UNITS - 2
TRIPS = (CHUNKS - 2) // 2

ACC = 0
PROJ = 2
UP = 4
UP0 = 0
SCORE = 4
PT = 6
OUT = 7
XT = 4

ROWS1 = slice(0, 256)
ROWS0 = slice(256, 384)
SW = 384


def bucket_starts():
    n = np.arange(SEQ)
    exact = BUCKETS // 2
    large = exact + (np.log(np.maximum(n, 1) / exact) / math.log(MAX_DIST / exact)
                     * (BUCKETS - exact)).astype(int)
    b = np.where(n < exact, n, np.minimum(large, BUCKETS - 1))
    return [int(np.argmax(b == i)) for i in range(BUCKETS)] + [SEQ]


def used_before_step(j):
    if j < HEADS - HG:
        return 3 + (3 * j) // HG
    return PROJ_UNITS + min(2, (j - (HEADS - HG)) // 2)


def split_plan():
    plan, done = [], 6
    for j in range(HEADS + 2):
        free = min(used_before_step(j) + SLOTS - 1, ATT_UNITS)
        plan.append(list(range(done, free)))
        done = max(done, free)
    assert done == ATT_UNITS
    return plan


def build(nc, x, rel_bias, w_qkv, w_o, ln_mix_g, ln_mix_b, w_up, w_down, ln_ffn_g, ln_ffn_b, out):
    F32, F32R = mybir.dt.float32, mybir.dt.float32r
    ACT = mybir.ActivationFunctionType
    ALU = mybir.AluOpType
    AX = mybir.AxisListType

    with ExitStack() as ctx:
        def sb(name, shape, dt=F32):
            return ctx.enter_context(nc.sbuf_tensor(name, shape, dt))

        def sem(name):
            return ctx.enter_context(nc.semaphore(name))

        w_raw = sb("w_raw", [P, SLOTS, UNIT])
        w_hi = sb("w_hi", [P, SLOTS, UNIT], F32R)
        w_lo = sb("w_lo", [P, SLOTS, UNIT], F32R)
        h = sb("h", [P, TT, D])
        xT_hi = sb("xT_hi", [P, KT, SEQ], F32R)
        xT_lo = sb("xT_lo", [P, KT, SEQ], F32R)
        xT32 = sb("xT32", [P, 2, SEQ])
        qkv_hi = sb("qkv_hi", [P, 2, 3, 512], F32R)
        qkv_lo = sb("qkv_lo", [P, 2, 3, 512], F32R)
        oT_hi = sb("oT_hi", [P, KT, SEQ], F32R)
        oT_lo = sb("oT_lo", [P, KT, SEQ], F32R)
        bias_rows = sb("bias_rows", [P, HEADS * SEQ])
        z = sb("z", [P, 2, SW])
        p = sb("p", [P, 2, SW])
        cum = sb("cum", [P, SW])
        pT_hi = sb("pT_hi", [P, 2, SW], F32R)
        pT_lo = sb("pT_lo", [P, 2, SW], F32R)
        relu = sb("relu", [P, 2, 512])
        u = sb("u", [P, 512])
        mask = sb("mask", [P, SW])
        ident = sb("ident", [P, P])
        relT = sb("relT", [HEADS, BUCKETS])
        by_dist = sb("by_dist", [HEADS, SW])
        gb_in = sb("gb_in", [8 * KT, P])
        gbT = sb("gbT", [P, 8 * KT])
        negmax = sb("negmax", [P, 2, 2])
        sums = sb("sums", [P, 2, 2])
        rinv = sb("rinv", [P, 2, 2])
        stats = sb("stats", [P, TT, 2, 6])
        mv = sb("mv", [P, TT, 2])
        v4 = sb("v4", [P, TT])
        lnv = sb("lnv", [P, TT])
        half_r0 = sb("half_r0", [P, TT])
        newton = sb("newton", [P, TT])
        norm_const = sb("norm_const", [P, 2])
        rstd = sb("rstd", [P, TT])
        nmr = sb("nmr", [P, 1])
        ps = ctx.enter_context(nc.psum_tensor("ps", [P, 8, 512], F32))
        dist_dram = nc.dram_tensor("dist_dram", (HEADS, SW), F32, kind="Internal")

        bias = bias_rows[:, :].rearrange("p (h k) -> p h k", h=HEADS)
        gb_rows = bias_rows[:, :].rearrange("p (a d) -> p a d", a=4)

        raw_loaded = [sem(f"raw_loaded{s}") for s in range(SLOTS)]
        hi_done = sem("hi_done")
        lo_done = sem("lo_done")
        unit_used = sem("unit_used")
        x_loaded = [sem(f"x_loaded{t}") for t in range(TT)]
        gb_loaded = sem("gb_loaded")
        rel_loaded = sem("rel_loaded")
        dist_stored = sem("dist_stored")
        bias_loaded = sem("bias_loaded")
        rows_loaded = sem("rows_loaded")
        out_stored = sem("out_stored")
        ident_ready = sem("ident_ready")
        mask_ready = sem("mask_ready")
        pool_own = sem("pool_own")
        dve_own = sem("dve_own")
        act_own = sem("act_own")
        gbT_psum = sem("gbT_psum")
        gbT_ready = sem("gbT_ready")
        xhat0_ready = sem("xhat0_ready")
        xhat1_ready = sem("xhat1_ready")
        xT_psum = sem("xT_psum")
        xT0_hi = sem("xT0_hi")
        xT0_ready = sem("xT0_ready")
        xT32_ready = sem("xT32_ready")
        xT_ready = sem("xT_ready")
        h_ready = sem("h_ready")
        norm_const_ready = sem("norm_const_ready")
        var_ready = sem("var_ready")
        half_r0_ready = sem("half_r0_ready")
        rstd_ready = sem("rstd_ready")
        piece_loaded = [sem(f"piece_loaded{q}") for q in range(4)]
        piece_hi = sem("piece_hi")
        piece_lo = sem("piece_lo")
        half_loaded = sem("half_loaded")
        half_hi = sem("half_hi")
        half_lo = sem("half_lo")
        qkv_hi_ready = sem("qkv_hi_ready")
        qkv_ready = sem("qkv_ready")
        score_done = sem("score_done")
        z_ready = sem("z_ready")
        logit_ready = sem("logit_ready")
        soft_done = sem("soft_done")
        exp_done = sem("exp_done")
        prob_ready = sem("prob_ready")
        pT_psum = sem("pT_psum")
        pT_hi_ready = sem("pT_hi_ready")
        pT_ready = sem("pT_ready")
        pv_done = sem("pv_done")
        oT_hi_ready = sem("oT_hi_ready")
        oT_ready = sem("oT_ready")
        relu_ready = sem("relu_ready")
        uT_ready = sem("uT_ready")
        acc_done = sem("acc_done")
        y_pool_ready = sem("y_pool_ready")
        y_dve_ready = sem("y_dve_ready")

        def f32(ap):
            return ap.bitcast(F32)

        class Own:
            def __init__(self, s):
                self.s, self.n, self.shift = s, 0, 0

            def mark(self, ins):
                ins.then_inc(self.s, 1)
                self.n += 1

            def wait(self, eng):
                eng.wait_ge(self.s, self.n + self.shift)

        def uT(t, c):
            return t[:, c % 2, 0, :].rearrange("p (k s) -> p k s", k=FC // P)

        SPLITS = split_plan()
        A_STEPS = HEADS + 2
        block = ctx.enter_context(nc.Block())

        @block.sync
        def _(sp):
            for t in range(TT):
                sp.dma_start(h[:, t, :], x[0, t * P:(t + 1) * P, :]).then_inc(x_loaded[t], 16)

            first = w_qkv[0].rearrange("(q k p) n -> q p k n", p=P, q=4)
            for q in range(4):
                sp.dma_start(w_raw[:, 0, q * 512:(q + 1) * 512].rearrange("p (k n) -> p k n", k=2),
                             first[q, :, :, 0:GC]).then_inc(piece_loaded[q], 16)

            second = w_qkv[0].rearrange("(q k p) n -> q p k n", p=P, q=2)
            for q in range(2):
                sp.dma_start(w_raw[:, 1, q * 1024:(q + 1) * 1024].rearrange("p (k n) -> p k n", k=KT // 2),
                             second[q, :, :, D:D + GC]).then_inc(raw_loaded[1] if q else half_loaded, 16)

            def load(n, slot, src, shape, always=False):
                if always or n >= SLOTS:
                    sp.wait_ge(lo_done, n - SLOTS + 1)
                dst = w_raw[:, slot, :].rearrange("p (k n) -> p k n", k=shape)
                sp.dma_start(dst, src).then_inc(raw_loaded[slot], 16)

            for l in range(DEPTH):
                n0 = l * LAYER_UNITS
                qkv_l = w_qkv[l].rearrange("(k p) (w n) -> p k w n", p=P, w=3)
                o_l = w_o[l].rearrange("(g k p) n -> p g k n", p=P, g=GROUPS)
                up_l = w_up[l].rearrange("(k p) n -> p k n", p=P)
                down_l = w_down[l].rearrange("(k p) n -> p k n", p=P)
                for m in range(2 if l == 0 else 0, PROJ_UNITS):
                    g, w = divmod(m, 3)
                    load(n0 + m, m % SLOTS, qkv_l[:, :, w, g * GC:(g + 1) * GC], KT)
                for g in range(GROUPS):
                    m = PROJ_UNITS + g
                    load(n0 + m, m % SLOTS, o_l[:, g], GC // P)

                def load_up(n, slot, c):
                    load(n, slot, up_l[:, :, bass.ds(c * FC, FC)], KT, True)

                def load_down(n, slot, c):
                    load(n, slot, down_l[:, bass.ds(c * (FC // P), FC // P), :], FC // P, True)

                f0 = n0 + ATT_UNITS
                load_up(f0, 0, 0)
                with sp.Fori(0, TRIPS) as i:
                    load_up(f0 + 1 + 4 * i, 1, 2 * i + 1)
                    load_down(f0 + 2 + 4 * i, 2, 2 * i)
                    load_up(f0 + 3 + 4 * i, 3, 2 * i + 2)
                    load_down(f0 + 4 + 4 * i, 0, 2 * i + 1)
                load_up(f0 + 29, 1, CHUNKS - 1)
                load_down(f0 + 30, 2, CHUNKS - 2)
                load_down(f0 + 31, 3, CHUNKS - 1)

            for t, s, ready, count in ((0, 1, y_dve_ready, 1), (0, 0, y_pool_ready, 1),
                                       (1, 0, y_dve_ready, 2), (1, 1, y_dve_ready, 3)):
                sp.wait_ge(ready, count)
                sp.dma_start(out[0, t * P:(t + 1) * P, HALVES[s]], h[:, t, HALVES[s]]).then_inc(out_stored, 16)
            sp.wait_ge(out_stored, 16 * 2 * TT)

        @block.gpsimd
        def _(pool):
            own = Own(pool_own)
            own.mark(pool.memset(ident[:, :], 0.0))
            own.wait(pool)
            pool.affine_select(out=ident[:, :], in_=ident[:, :], compare_op=ALU.not_equal, fill=1.0,
                               base=0, pattern=[[-1, P]], channel_multiplier=1).then_inc(ident_ready, 1)
            pool.dma_start(relT[:, :], rel_bias.rearrange("b h -> h b"),
                           allow_slow_non_contiguous=True).then_inc(rel_loaded, 16)
            pool.memset(norm_const[:, 0:1], EPS).then_inc(norm_const_ready, 1)
            pool.memset(norm_const[:, 1:2], -math.log(2.0)).then_inc(norm_const_ready, 1)
            own.mark(pool.memset(by_dist[:, :], -BIG))
            own.mark(pool.memset(mask[:, :], 0.0))
            own.wait(pool)
            diag = mask[:, P:SW].rearrange("p (a k) -> p a k", a=2)
            pool.affine_select(out=diag, in_=diag, compare_op=ALU.is_gt, fill=-BIG,
                               base=0, pattern=[[0, 2], [-1, P]], channel_multiplier=1).then_inc(mask_ready, 1)
            pool.wait_ge(rel_loaded, 16)
            starts = bucket_starts()
            exact = BUCKETS // 2
            own.mark(pool.tensor_copy(by_dist[:, P - 1:P - 1 + exact], relT[:, 0:exact]))
            for b in range(exact, BUCKETS):
                lo, hi = starts[b], starts[b + 1]
                own.mark(pool.tensor_copy(by_dist[:, P - 1 + lo:P - 1 + hi],
                                          relT[:, b:b + 1].to_broadcast([HEADS, hi - lo])))
            own.wait(pool)
            pool.dma_start(dist_dram.ap(), by_dist[:, :]).then_inc(dist_stored, 16)
            pool.wait_ge(dist_stored, 16)
            pool.dma_start(bias, bass.AP(dist_dram, 0, [[1, P], [SW, HEADS], [1, SEQ]])).then_inc(bias_loaded, 16)

            def split_lo(n, slot):
                pool.wait_ge(hi_done, n)
                pool.wait_ge(lo_done, n)
                pool.tensor_tensor(w_lo[:, slot, :], w_raw[:, slot, :], f32(w_hi[:, slot, :]),
                                   ALU.subtract).then_inc(lo_done, 1)

            for l in range(DEPTH):
                for m in range(POOL_FIRST, ATT_UNITS + 2):
                    split_lo(l * LAYER_UNITS + m, m % SLOTS)
                if l == 0:
                    pool.wait_ge(z_ready, HEADS)
                else:
                    pool.wait_ge(h_ready, 2 * TT)
                for a, v in enumerate((ln_mix_g, ln_mix_b, ln_ffn_g, ln_ffn_b)):
                    pool.dma_start(gb_rows[:, a, :], bass.AP(v.tensor, l * D, [[0, P], [1, D]])).then_inc(rows_loaded, 16)
                pool.wait_ge(rows_loaded, 64 * (l + 1))
                for s in range(2):
                    ln = 2 * l + s + 1
                    if ln == 2 * DEPTH:
                        y00 = h[:, 0, HALVES[0]]
                        pool.wait_ge(xhat0_ready, 2 * (ln - 1) + 1)
                        own.mark(pool.tensor_tensor(y00, y00, gb_rows[:, 2, HALVES[0]], ALU.mult))
                        own.wait(pool)
                        pool.tensor_tensor(y00, y00, gb_rows[:, 3, HALVES[0]], ALU.add).then_inc(y_pool_ready, 1)
                        break
                    if s == 1:
                        split_lo((l + 1) * LAYER_UNITS + 1, 1)
                    pool.wait_ge(xT_psum, 4 * (ln + 1))
                    for t in range(TT):
                        own.mark(pool.tensor_tensor(h[:, t, :], h[:, t, :], gb_rows[:, 2 * s, :], ALU.mult))
                        own.wait(pool)
                        pool.tensor_tensor(h[:, t, :], h[:, t, :], gb_rows[:, 2 * s + 1, :],
                                           ALU.add).then_inc(h_ready, 1)

        @block.scalar
        def _(act):
            own = Own(act_own)
            act.preload_act_table_set("natural_log_exp_and_others")
            for a, v in enumerate((ln_mix_g, ln_mix_b, ln_ffn_g, ln_ffn_b)):
                act.dma_start(gb_in[a * 2 * KT:(a + 1) * 2 * KT, :],
                              v.rearrange("l (k p) -> (l k) p", p=P)).then_inc(gb_loaded, 16)

            def split_hi(n, slot, always=False, uses=None):
                act.wait_ge(raw_loaded[slot], uses if uses is not None else 16 * (n // SLOTS + (slot > 0)))
                if always or n >= SLOTS:
                    act.wait_ge(unit_used, n - SLOTS + 1)
                act.copy(w_hi[:, slot, :], w_raw[:, slot, :]).then_inc(hi_done, 1)

            def split_piece(q):
                act.wait_ge(piece_loaded[q], 16)
                part = slice(q * 512, (q + 1) * 512)
                act.copy(w_hi[:, 0, part], w_raw[:, 0, part]).then_inc(piece_hi, 1)

            def xT_evac(ln):
                if ln == 0:
                    for q in range(KT // 2):
                        act.wait_ge(xT_psum, q + 1)
                        act.copy(xT_hi[:, 2 * q:2 * q + 2, :].rearrange("p k s -> p (k s)"),
                                 ps[:, XT + q, :]).then_inc(xT0_hi, 1)
                        split_piece(q)
                    return
                for k in range(KT):
                    if k % 2 == 0:
                        act.wait_ge(xT_psum, 4 * ln + k // 2 + 1)
                    if k >= 2 or ln >= 2:
                        act.wait_ge(xT_ready, 8 * (ln - 1) + k - 1)
                    src = ps[:, XT + k // 2, (k % 2) * SEQ:(k % 2 + 1) * SEQ]
                    if ln == 1 and k == 0:
                        act.wait_ge(gbT_ready, 1)
                    l, s = divmod(ln - 1, 2)
                    col = 4 * s * KT + l * KT + k
                    gain, offs = gbT[:, col:col + 1], gbT[:, col + 2 * KT:col + 2 * KT + 1]
                    act.activation(xT32[:, k % 2, :], src, ACT.Identity, bias=offs,
                                   scale=gain).then_inc(xT32_ready, 1)

            def ln_rstd(ln):
                for t in range(TT):
                    if ln == 1 and t == 0:
                        act.wait_ge(norm_const_ready, 2)
                    act.wait_ge(var_ready, TT * (ln - 1) + t + 1)
                    own.mark(act.activation(lnv[:, t:t + 1], mv[:, t, 1:2], ACT.Ln, bias=norm_const[:, 0:1]))
                    own.wait(act)
                    act.activation(half_r0[:, t:t + 1], lnv[:, t:t + 1], ACT.Exp, scale=-0.5,
                                   bias=norm_const[:, 1:2]).then_inc(half_r0_ready, 1)
                    if t == 0:
                        act.wait_ge(rstd_ready, ln)
                        for c in range(2 if ln < 2 * DEPTH else 1):
                            half = h[:, 0, HALVES[c]]
                            act.activation(half, half, ACT.Identity, bias=nmr[:, :],
                                           scale=rstd[:, 0:1]).then_inc(xhat0_ready, 1)

            def qkv_evac(l, g, w):
                m = 3 * g + w
                act.wait_ge(unit_used, LAYER_UNITS * l + m + 1)
                if g >= 2:
                    act.wait_ge(pv_done, (HEADS * l + HG * (g - 1)) // 2)
                act.activation(qkv_hi[:, g % 2, w, :], ps[:, PROJ + m % 2, :], ACT.Copy,
                               scale=QK_SCALE if w == 0 else 1.0).then_inc(qkv_hi_ready, 1)

            def exp_part(l, j):
                hd = HEADS * l + j
                zj, pj = z[:, j % 2, :], p[:, j % 2, :]
                act.wait_ge(logit_ready, hd + 1)
                if l == 0:
                    if j >= 2:
                        act.wait_ge(pT_psum, hd - 1)
                    act.activation(pj[:, ROWS1], zj[:, ROWS1], ACT.Exp, bias=negmax[:, j % 2, 0:1],
                                   accum_out=sums[:, j % 2, 0:1])
                    act.activation(pj[:, ROWS0], zj[:, ROWS0], ACT.Exp, bias=negmax[:, j % 2, 1:2],
                                   accum_out=sums[:, j % 2, 1:2]).then_inc(exp_done, 1)
                else:
                    act.activation(pj, zj, ACT.Exp).then_inc(exp_done, 1)

            def softplus_part(l, j):
                hd = HEADS * l + j
                zj, pj = z[:, j % 2, :], p[:, j % 2, :]
                act.wait_ge(z_ready, hd + 1)
                act.wait_ge(pT_psum, hd - 1)
                if j >= 2:
                    act.wait_ge(logit_ready, hd - 1)
                act.activation(relu[:, j % 2, 0:SW], zj, ACT.Relu)
                own.mark(act.activation(pj, zj, ACT.Abs))
                own.wait(act)
                own.mark(act.activation(pj, pj, ACT.Exp, scale=-1.0))
                own.wait(act)
                act.activation(pj, pj, ACT.Ln, bias=1.0).then_inc(soft_done, 1)

            def pT_evac(l, j):
                hd = HEADS * l + j
                act.wait_ge(pT_psum, hd + 1)
                if j >= 2:
                    act.wait_ge(pv_done, hd // 2)
                act.copy(pT_hi[:, j % 2, :], ps[:, PT, 0:SW]).then_inc(pT_hi_ready, 1)

            def o_evac(l, pair):
                act.wait_ge(pv_done, HEADS // 2 * l + pair + 1)
                for r in range(2):
                    rows, cols = slice(DH * r, DH * (r + 1)), slice(SEQ * r, SEQ * (r + 1))
                    act.copy(oT_hi[rows, pair, :], ps[rows, OUT, cols]).then_inc(oT_hi_ready, 1)

            def relu_evac(k, l, c, first=False):
                act.wait_ge(unit_used, LAYER_UNITS * l + ATT_UNITS + (1 if first else 2 * c))
                if not first:
                    act.wait_ge(uT_ready, CHUNKS * l + c)
                act.activation(relu[:, k, :], ps[:, UP0 if first else UP + k, :], ACT.Relu).then_inc(relu_ready, 1)

            xT_evac(0)
            act.wait_ge(half_loaded, 16)
            act.copy(w_hi[:, 1, 0:UNIT // 2], w_raw[:, 1, 0:UNIT // 2]).then_inc(half_hi, 1)
            act.wait_ge(raw_loaded[1], 16)
            act.copy(w_hi[:, 1, UNIT // 2:UNIT], w_raw[:, 1, UNIT // 2:UNIT]).then_inc(hi_done, 1)
            split_hi(2, 2)
            for l in range(DEPTH):
                n0 = l * LAYER_UNITS
                qkv_evac(l, 0, 0)
                if l == 0:
                    split_hi(3, 3)
                qkv_evac(l, 0, 1)
                split_hi(n0 + 4, 0)
                split_hi(n0 + 5, 1)
                qkv_evac(l, 0, 2)
                evac = 3
                for j in range(A_STEPS):
                    if l == 1 and j >= 2:
                        pT_evac(l, j - 2)
                    for m in SPLITS[j]:
                        split_hi(n0 + m, m % SLOTS)
                    if l == 0 and j == HEADS:
                        split_hi(n0 + ATT_UNITS, 0)
                    if l == 0:
                        if j < HEADS:
                            exp_part(l, j)
                        if 1 <= j <= HEADS:
                            pT_evac(l, j - 1)
                    else:
                        if 1 <= j <= HEADS:
                            exp_part(l, j - 1)
                        if j < HEADS:
                            softplus_part(l, j)
                    while evac < min(PROJ_UNITS, used_before_step(j + 1)):
                        qkv_evac(l, evac // 3, evac % 3)
                        evac += 1
                    if l == 1 and j == HEADS + 1:
                        split_hi(n0 + ATT_UNITS, 0)
                    if j >= 3 and j % 2 == 1:
                        o_evac(l, (j - 3) // 2)
                    if l == 0 and j == HEADS:
                        split_hi(n0 + ATT_UNITS + 1, 1)
                if l == 1:
                    split_hi(n0 + ATT_UNITS + 1, 1)
                ln_rstd(2 * l + 1)
                xT_evac(2 * l + 1)
                split_hi(n0 + ATT_UNITS + 2, 2)

                f0 = n0 + ATT_UNITS
                relu_evac(0, l, 0, first=True)
                r0 = 16 * (f0 // SLOTS)
                with act.Fori(0, TRIPS) as i:
                    split_hi(f0 + 3 + 4 * i, 3, True, r0 + 16 + 16 * i)
                    split_hi(f0 + 4 + 4 * i, 0, True, r0 + 16 + 16 * i)
                    relu_evac(1, l, 2 * i + 1)
                    split_hi(f0 + 5 + 4 * i, 1, True, r0 + 32 + 16 * i)
                    split_hi(f0 + 6 + 4 * i, 2, True, r0 + 32 + 16 * i)
                    relu_evac(0, l, 2 * i + 2)
                split_hi(f0 + 31, 3)
                if l + 1 < DEPTH:
                    split_hi(f0 + 32, 0)
                relu_evac(1, l, CHUNKS - 1)
                if l + 1 < DEPTH:
                    split_hi(f0 + 33, 1)
                ln_rstd(2 * l + 2)
                if l + 1 < DEPTH:
                    xT_evac(2 * l + 2)
                    split_hi(f0 + 34, 2)
                    split_hi(f0 + 35, 3)

        @block.vector
        def _(dve):
            own = Own(dve_own)

            def split_lo(n, slot):
                dve.wait_ge(hi_done, n)
                dve.tensor_tensor(w_lo[:, slot, :], w_raw[:, slot, :], f32(w_hi[:, slot, :]),
                                  ALU.subtract).then_inc(lo_done, 1)

            def split_piece(q):
                dve.wait_ge(piece_hi, q + 1)
                part = slice(q * 512, (q + 1) * 512)
                dve.tensor_tensor(w_lo[:, 0, part], w_raw[:, 0, part], f32(w_hi[:, 0, part]),
                                  ALU.subtract).then_inc(piece_lo if q < 3 else lo_done, 1)

            def xT_evac(ln):
                if ln == 0:
                    for q in range(KT // 2):
                        pair = [t[:, 2 * q:2 * q + 2, :].rearrange("p k s -> p (k s)") for t in (xT_hi, xT_lo)]
                        dve.wait_ge(xT0_hi, q + 1)
                        dve.tensor_tensor(pair[1], ps[:, XT + q, :], f32(pair[0]),
                                          ALU.subtract).then_inc(xT0_ready, 1)
                        split_piece(q)
                    return
                for k in range(KT):
                    dve.wait_ge(xT32_ready, 8 * (ln - 1) + k + 1)
                    own.mark(dve.tensor_copy(xT_hi[:, k, :], xT32[:, k % 2, :]))
                    own.wait(dve)
                    dve.tensor_tensor(xT_lo[:, k, :], xT32[:, k % 2, :], f32(xT_hi[:, k, :]),
                                      ALU.subtract).then_inc(xT_ready, 1)

            def norm(ln):
                def add(t, s):
                    hs = h[:, t, HALVES[s]]
                    if t == 0 and s == 0 and ln >= 2:
                        dve.wait_ge(h_ready, TT * (ln - 1))
                    if 2 * t + s < ACC_PARTS:
                        dve.wait_ge(acc_done, ACC_PARTS * (ln - 1) + 2 * t + s + 1)
                    else:
                        l, ffn = divmod(ln - 1, 2)
                        dve.wait_ge(unit_used, LAYER_UNITS * l + (LAYER_UNITS if ffn else ATT_UNITS))
                    own.mark(dve.scalar_tensor_tensor(hs, hs, ALPHA, ps[:, ACC + 2 * t + s, :],
                                                      ALU.mult, ALU.add))

                def measure(t, s):
                    own.wait(dve)
                    own.mark(dve.bn_stats(stats[:, t, s, :], h[:, t, HALVES[s]]))

                def variance(t):
                    own.wait(dve)
                    dve.bn_aggr(mv[:, t, :], stats[:, t, :, :]).then_inc(var_ready, 1)
                    dve.wait_ge(var_ready, TT * (ln - 1) + t + 1)
                    own.mark(dve.tensor_scalar(v4[:, t:t + 1], mv[:, t, 1:2], EPS, -4.0, ALU.add, ALU.mult))

                def inverse_root(t):
                    dve.wait_ge(half_r0_ready, TT * (ln - 1) + t + 1)
                    own.wait(dve)
                    r = half_r0[:, t:t + 1]
                    own.mark(dve.scalar_tensor_tensor(newton[:, t:t + 1], r, v4[:, t:t + 1], r, ALU.mult, ALU.mult))
                    own.wait(dve)
                    own.mark(dve.scalar_tensor_tensor(rstd[:, t:t + 1], newton[:, t:t + 1], 3.0, r,
                                                      ALU.add, ALU.mult))
                    if t == 0:
                        own.wait(dve)
                        dve.scalar_tensor_tensor(nmr[:, :], mv[:, 0, 0:1], -1.0, rstd[:, 0:1],
                                                 ALU.mult, ALU.mult).then_inc(rstd_ready, 1)

                def centre(t, s):
                    row = h[:, t, HALVES[s]]
                    own.mark(dve.scalar_tensor_tensor(row, row, mv[:, t, 0:1], gb_rows[:, 2, HALVES[s]],
                                                      ALU.subtract, ALU.mult))

                def scale(t, s):
                    row = h[:, t, HALVES[s]]
                    dve.scalar_tensor_tensor(row, row, rstd[:, t:t + 1], gb_rows[:, 3, HALVES[s]],
                                             ALU.mult, ALU.add).then_inc(y_dve_ready, 1)

                def xhat1(cols):
                    row = h[:, 1, cols]
                    dve.tensor_scalar(row, row, mv[:, 1, 0:1], rstd[:, 1:2],
                                      ALU.subtract, ALU.mult).then_inc(xhat1_ready, 1)

                output = ln == 2 * DEPTH
                if output:
                    dve.wait_ge(rows_loaded, 64 * DEPTH)
                add(0, 0)
                measure(0, 0)
                add(0, 1)
                measure(0, 1)
                variance(0)
                if output:
                    centre(0, 1)
                add(1, 0)
                inverse_root(0)
                measure(1, 0)
                if output:
                    scale(0, 1)
                add(1, 1)
                measure(1, 1)
                variance(1)
                if output:
                    centre(1, 0)
                inverse_root(1)
                own.wait(dve)
                if output:
                    scale(1, 0)
                    centre(1, 1)
                    own.wait(dve)
                    scale(1, 1)
                else:
                    for cols in XHAT1_PARTS:
                        xhat1(cols)

            def qkv_evac(l, g, w):
                m = 3 * g + w
                dve.wait_ge(qkv_hi_ready, PROJ_UNITS * l + m + 1)
                dve.scalar_tensor_tensor(qkv_lo[:, g % 2, w, :], ps[:, PROJ + m % 2, :],
                                         QK_SCALE if w == 0 else 1.0, f32(qkv_hi[:, g % 2, w, :]),
                                         ALU.mult, ALU.subtract).then_inc(qkv_ready, 1)

            def scores(l, j):
                hd = HEADS * l + j
                s, zj = ps[:, SCORE + j % 2, 0:SW], z[:, j % 2, :]
                dve.wait_ge(score_done, hd + 1)
                if hd >= 2:
                    dve.wait_ge(exp_done, hd - 1)
                if l == 0:
                    if j == 0:
                        dve.wait_ge(bias_loaded, 16)
                    rev = bass.AP(bias_rows, j * SEQ + SEQ - 1, [[HEADS * SEQ, P], [-1, SEQ]])
                    rev0 = bass.AP(bias_rows, j * SEQ + P - 1, [[HEADS * SEQ, P], [-1, P]])
                    own.mark(dve.scalar_tensor_tensor(zj[:, ROWS1], s[:, ROWS1], 1.0, rev, ALU.mult, ALU.add))
                    dve.scalar_tensor_tensor(zj[:, ROWS0], s[:, ROWS0], 1.0, rev0, ALU.mult,
                                             ALU.add).then_inc(z_ready, 1)
                    own.wait(dve)
                    dve.reduce_max(negmax[:, j % 2, 0:1], zj[:, ROWS1], AX.X, negate=True)
                    dve.wait_ge(z_ready, hd + 1)
                    dve.reduce_max(negmax[:, j % 2, 1:2], zj[:, ROWS0], AX.X, negate=True).then_inc(logit_ready, 1)
                else:
                    if j == 0:
                        dve.wait_ge(mask_ready, 1)
                    dve.scalar_tensor_tensor(zj, s, 1.0, mask[:, :], ALU.mult, ALU.add).then_inc(z_ready, 1)

            def normalise(l, j):
                hd = HEADS * l + j
                dve.wait_ge(exp_done, hd + 1)
                own.mark(dve.reciprocal(rinv[:, j % 2, :], sums[:, j % 2, :]))
                own.wait(dve)
                for i, rows in enumerate((ROWS1, ROWS0)):
                    pj = p[:, j % 2, rows]
                    dve.tensor_scalar(pj, pj, rinv[:, j % 2, i:i + 1], None, ALU.mult).then_inc(prob_ready, 1)

            def stick(l, j):
                hd = HEADS * l + j
                zj, pj = z[:, j % 2, :], p[:, j % 2, :]
                dve.wait_ge(soft_done, j + 1)
                for rows in (ROWS1, ROWS0):
                    n = rows.stop - rows.start
                    back = bass.AP(p, (j % 2) * SW + rows.stop - 1, [[2 * SW, P], [-1, n]])
                    back_relu = bass.AP(relu, (j % 2) * 512 + rows.stop - 1, [[2 * 512, P], [-1, n]])
                    back_sum = bass.AP(cum, rows.stop - 1, [[SW, P], [-1, n]])
                    own.mark(dve.tensor_tensor_scan(back_sum, back_relu, back, 0.0, ALU.add, ALU.add))
                own.wait(dve)
                dve.tensor_tensor(zj, zj, cum[:, :], ALU.subtract).then_inc(logit_ready, 1)

            def pT_evac(l, j):
                hd = HEADS * l + j
                dve.wait_ge(pT_hi_ready, hd + 1)
                dve.tensor_tensor(pT_lo[:, j % 2, :], ps[:, PT, 0:SW], f32(pT_hi[:, j % 2, :]),
                                  ALU.subtract).then_inc(pT_ready, 1)

            def o_evac(l, pair):
                for r in range(2):
                    rows, cols = slice(DH * r, DH * (r + 1)), slice(SEQ * r, SEQ * (r + 1))
                    dve.wait_ge(oT_hi_ready, HEADS * l + 2 * pair + r + 1)
                    dve.tensor_tensor(oT_lo[rows, pair, :], ps[rows, OUT, cols], f32(oT_hi[rows, pair, :]),
                                      ALU.subtract).then_inc(oT_ready, 1)

            def square(k, l, c):
                dve.wait_ge(relu_ready, CHUNKS * l + c + 1)
                own.mark(dve.tensor_tensor(u[:, :], relu[:, k, :], relu[:, k, :], ALU.mult))
                own.wait(dve)
                own.mark(dve.tensor_copy(qkv_hi[:, k, 0, :], u[:, :]))
                own.wait(dve)
                dve.tensor_tensor(qkv_lo[:, k, 0, :], u[:, :], f32(qkv_hi[:, k, 0, :]),
                                  ALU.subtract).then_inc(uT_ready, 1)

            xT_evac(0)
            for q in range(2):
                half = slice(q * UNIT // 2, (q + 1) * UNIT // 2)
                dve.wait_ge(hi_done if q else half_hi, 1)
                dve.tensor_tensor(w_lo[:, 1, half], w_raw[:, 1, half], f32(w_hi[:, 1, half]),
                                  ALU.subtract).then_inc(lo_done if q else half_lo, 1)
            split_lo(2, 2)
            for l in range(DEPTH):
                n0 = l * LAYER_UNITS
                qkv_evac(l, 0, 0)
                if l == 0:
                    split_lo(3, 3)
                    dve.wait_ge(gbT_psum, 1)
                    dve.tensor_copy(gbT[:, :], ps[:, OUT, 0:8 * KT]).then_inc(gbT_ready, 1)
                qkv_evac(l, 0, 1)
                split_lo(n0 + 4, 0)
                split_lo(n0 + 5, 1)
                qkv_evac(l, 0, 2)
                evac = 3
                for j in range(A_STEPS):
                    if j < HEADS:
                        scores(l, j)
                    if l == 1:
                        if 1 <= j <= HEADS:
                            stick(l, j - 1)
                        if j >= 2:
                            pT_evac(l, j - 2)
                        if j >= 4 and j % 2 == 0:
                            o_evac(l, (j - 4) // 2)
                    for m in SPLITS[j]:
                        if m < POOL_FIRST:
                            split_lo(n0 + m, m % SLOTS)
                    if l == 0:
                        if 1 <= j <= HEADS:
                            pT_evac(l, j - 1)
                        if j < HEADS:
                            normalise(l, j)
                    while evac < min(PROJ_UNITS, used_before_step(j + 1)):
                        qkv_evac(l, evac // 3, evac % 3)
                        evac += 1
                    if l == 0 and j >= 3 and j % 2 == 1:
                        o_evac(l, (j - 3) // 2)
                if l == 1:
                    o_evac(l, HEADS // 2 - 1)
                norm(2 * l + 1)
                xT_evac(2 * l + 1)
                dve.wait_ge(lo_done, n0 + ATT_UNITS + 2)
                split_lo(n0 + ATT_UNITS + 2, 2)

                f0 = n0 + ATT_UNITS
                square(0, l, 0)
                per_trip, start = 4, own.n
                with dve.Fori(0, TRIPS) as i:
                    own.shift = per_trip * i
                    split_lo(f0 + 3 + 4 * i, 3)
                    split_lo(f0 + 4 + 4 * i, 0)
                    square(1, l, 2 * i + 1)
                    split_lo(f0 + 5 + 4 * i, 1)
                    split_lo(f0 + 6 + 4 * i, 2)
                    square(0, l, 2 * i + 2)
                assert own.n == start + per_trip
                own.n, own.shift = start + per_trip * TRIPS, 0
                split_lo(f0 + 31, 3)
                if l + 1 < DEPTH:
                    split_lo(f0 + 32, 0)
                square(1, l, CHUNKS - 1)
                norm(2 * l + 2)
                if l + 1 < DEPTH:
                    xT_evac(2 * l + 2)
                    dve.wait_ge(lo_done, f0 + 34)
                    split_lo(f0 + 34, 2)
                    split_lo(f0 + 35, 3)

        @block.tensor
        def _(pe):
            PASSES = ((0, 0), (0, 1), (1, 0))
            xT, w, qkv, oT, pT = (xT_hi, xT_lo), (w_hi, w_lo), (qkv_hi, qkv_lo), (oT_hi, oT_lo), (pT_hi, pT_lo)

            def stay_warm(n):
                for _ in range(n):
                    pe.transpose(ps[:, ACC, 0:P], ident[:, :], ident[:, :])

            def transposes(ln):
                for t in range(TT):
                    if t == 1 and ln >= 1:
                        stay_warm(10)
                    for k in range(KT):
                        if ln == 0 and k == 0:
                            pe.wait_ge(x_loaded[t], 16)
                        if ln >= 1 and t == 0 and k % 4 == 0:
                            pe.wait_ge(xhat0_ready, 2 * (ln - 1) + k // 4 + 1)
                        if ln >= 1 and t == 1 and k in (0, 2, 4):
                            pe.wait_ge(xhat1_ready, 3 * (ln - 1) + k // 2 + 1)
                        o = (k % 2) * SEQ + t * P
                        mm = pe.transpose(ps[:, XT + k // 2, o:o + P], h[:, t, k * P:(k + 1) * P], ident[:, :])
                        if t == TT - 1 and k % 2 == 1:
                            mm.then_inc(xT_psum, 1)

            def feature_major(slot, bank, k, ln):
                wk = [t[:, slot, :].rearrange("p (k n) -> p k n", k=KT) for t in w]
                if ln == 0:
                    if k % 2 == 0:
                        pe.wait_ge(xT0_ready, k // 2 + 1)
                elif ln is not None:
                    pe.wait_ge(xT_ready, 8 * (ln - 1) + k + 1)
                for c in range(2):
                    for i, (a, b) in enumerate(PASSES):
                        mm = pe.matmul(ps[:, bank, c * SEQ:(c + 1) * SEQ], wk[a][:, k, c * P:(c + 1) * P],
                                       xT[b][:, k, :], start=(k == 0 and c == 0 and i == 0),
                                       stop=(k == KT - 1 and i == 2), skip_group_check=True)
                return mm

            def token_major(slot, bank, k):
                wk = [t[:, slot, :].rearrange("p (k n) -> p k n", k=KT) for t in w]
                for t in range(TT):
                    for i, (a, b) in enumerate(PASSES):
                        mm = pe.matmul(ps[:, bank, t * GC:(t + 1) * GC], xT[a][:, k, t * P:(t + 1) * P],
                                       wk[b][:, k, :], start=(k == 0 and t == 0 and i == 0),
                                       stop=(k == KT - 1 and i == 2), skip_group_check=True)
                return mm

            def proj(l, m, k):
                g, which = divmod(m, 3)
                n = l * LAYER_UNITS + m
                if n == 0 and k % 2 == 0 and k < KT - 2:
                    pe.wait_ge(piece_lo, k // 2 + 1)
                if n == 1 and k == 0:
                    pe.wait_ge(half_lo, 1)
                if k == {0: KT - 2, 1: KT // 2}.get(n, 0):
                    pe.wait_ge(lo_done, n + 1)
                if k == 0:
                    if m >= 2:
                        pe.wait_ge(qkv_ready, PROJ_UNITS * l + m - 1)
                if which < 2:
                    mm = feature_major(m % SLOTS, PROJ + m % 2, k, 2 * l if m == 0 else None)
                else:
                    mm = token_major(m % SLOTS, PROJ + m % 2, k)
                if k == KT - 1:
                    mm.then_inc(unit_used, 1)

            def sum_part(slot, src, k_src, k, t, first, last, parts=HALVES):
                wk = [x[:, slot, :].rearrange("p (k n) -> p k n", k=FC // P) for x in w]
                for cols in parts:
                    for i, (a, b) in enumerate(PASSES):
                        mm = pe.matmul(ps[:, ACC + 2 * t + cols.start // 512, :], src[a][:, k_src, t * P:(t + 1) * P],
                                       wk[b][:, k, cols], start=(first and i == 0), stop=(last and i == 2))
                return mm

            def o_slice(l, g, k, t, parts=HALVES, last=False, used=False):
                pe.wait_ge(lo_done, l * LAYER_UNITS + PROJ_UNITS + g + 1)
                pe.wait_ge(oT_ready, HEADS * l + HG * g + 2 * (k + 1))
                if t == 1:
                    pe.wait_ge(qkv_ready, PROJ_UNITS * (l + 1))
                mm = sum_part((PROJ_UNITS + g) % SLOTS, oT, 2 * g + k, k, t, g == 0 and k == 0, last, parts)
                if used:
                    mm.then_inc(unit_used, 1)
                return mm

            def o_finish(l):
                o_slice(l, 2, 0, 1)
                for cols in HALVES:
                    o_slice(l, 3, 1, 0, (cols,), last=True).then_inc(acc_done, 1)
                for cols in HALVES:
                    final = cols.stop == D
                    o_slice(l, 2, 1, 1, (cols,), used=final)
                    o_slice(l, 3, 0, 1, (cols,))
                    o_slice(l, 3, 1, 1, (cols,), last=True).then_inc(unit_used if final else acc_done, 1)

            def last_units(units):
                for slot, src, k0, waits in units:
                    for which, count in waits:
                        pe.wait_ge(which, count)
                    final = slot == units[-1][0]
                    for cols in HALVES:
                        for k in range(2):
                            mm = sum_part(slot, src, k0 + k, k, 0, False, final and k == 1, (cols,))
                        if final:
                            mm.then_inc(acc_done, 1)
                for cols in HALVES:
                    for slot, src, k0, _ in units:
                        final = slot == units[-1][0]
                        for k in range(2):
                            mm = sum_part(slot, src, k0 + k, k, 1, False, final and k == 1, (cols,))
                        if cols.stop == D:
                            mm.then_inc(unit_used, 1)
                    if cols.stop < D:
                        mm.then_inc(acc_done, 1)

            def attend_scores(l, j):
                hd = HEADS * l + j
                par, tile, r0 = (j // HG) % 2, (j % HG) // 2, DH * (j % 2)
                if j % HG == 0:
                    pe.wait_ge(qkv_ready, PROJ_UNITS * l + 3 * (j // HG) + 2)
                if j >= 2:
                    pe.wait_ge(z_ready, hd - 1)
                q = [t[r0:r0 + DH, par, 0, tile * SEQ:(tile + 1) * SEQ] for t in qkv]
                kk = [t[r0:r0 + DH, par, 1, tile * SEQ:(tile + 1) * SEQ] for t in qkv]
                for cols, t, nk in ((ROWS1, 1, SEQ), (ROWS0, 0, P)):
                    for i, (a, b) in enumerate(PASSES):
                        mm = pe.matmul(ps[:, SCORE + j % 2, cols], q[a][:, t * P:(t + 1) * P], kk[b][:, 0:nk],
                                       start=(i == 0), stop=(i == 2))
                mm.then_inc(score_done, 1)

            def attend_transpose(l, j):
                hd = HEADS * l + j
                if l == 0:
                    pe.wait_ge(prob_ready, 2 * (j + 1))
                else:
                    pe.wait_ge(exp_done, hd + 1)
                if hd >= 1:
                    pe.wait_ge(pT_ready, hd)
                pj = p[:, j % 2, :]
                for dst, src in ((0, 256), (128, 0), (256, 128)):
                    mm = pe.transpose(ps[:, PT, dst:dst + P], pj[:, src:src + P], ident[:, :])
                mm.then_inc(pT_psum, 1)

            def attend_values(l, pair):
                j = 2 * pair
                par = (j // HG) % 2
                pe.wait_ge(pT_ready, HEADS * l + j + 2)
                if j % HG == 0:
                    pe.wait_ge(qkv_ready, PROJ_UNITS * l + 3 * (j // HG) + 3)
                if l + pair > 0:
                    pe.wait_ge(oT_ready, HEADS * l + j)
                both = ps[:, OUT, :].rearrange("p (r s) -> p r s", r=2)
                for kt, dst, src in ((0, slice(0, SEQ), slice(0, SEQ)), (1, slice(P, SEQ), slice(SEQ, SW))):
                    for i, (a, b) in enumerate(PASSES):
                        c = kt * GC + (pair % 2) * P
                        mm = pe.matmul(both[:, :, dst], qkv[a][:, par, 2, c:c + P], pT[b][:, :, src],
                                       start=(kt == 0 and i == 0), stop=(kt == 1 and i == 2))
                mm.then_inc(pv_done, 1)

            def up(l, c, n, slot, bank, ln=None, wait_bank=True):
                pe.wait_ge(lo_done, n + 1)
                if wait_bank:
                    pe.wait_ge(relu_ready, CHUNKS * l + c - 1)
                for k in range(KT):
                    mm = feature_major(slot, bank, k, ln)
                mm.then_inc(unit_used, 1)

            def down(l, c, n, slot, par, first=False):
                pe.wait_ge(lo_done, n + 1)
                pe.wait_ge(uT_ready, CHUNKS * l + c + 1)
                src = [uT(t, par) for t in qkv]
                for k in range(2):
                    for t in range(TT):
                        mm = sum_part(slot, src, k, k, t, first and k == 0, False)
                mm.then_inc(unit_used, 1)

            pe.wait_ge(ident_ready, 1)
            stay_warm(12)
            for l in range(DEPTH):
                transposes(2 * l)
                for m in range(3):
                    for k in range(KT):
                        proj(l, m, k)
                    if l == 0 and m == 0:
                        pe.wait_ge(gb_loaded, 64)
                        pe.transpose(ps[:, OUT, 0:8 * KT], gb_in[:, :],
                                     ident[0:8 * KT, 0:8 * KT]).then_inc(gbT_psum, 1)
                ksteps = iter([(m, k) for m in range(3, PROJ_UNITS) for k in range(KT)])
                slices = iter([(g, k, t) for g in range(2) for k in range(2) for t in range(TT)] +
                              [(2, 0, 0), (2, 1, 0), (3, 0, 0)])
                for j in range(A_STEPS):
                    def fill():
                        if j < HEADS - HG:
                            for _ in range(2):
                                proj(l, *next(ksteps))
                        else:
                            part = next(slices, None)
                            if part is not None:
                                o_slice(l, *part, used=part[1:] == (1, 1))
                    odd = j >= 3 and j % 2 == 1
                    if l == 0:
                        fill()
                        if j < HEADS:
                            attend_scores(l, j)
                        if j <= HEADS:
                            fill()
                        if odd:
                            attend_values(l, (j - 3) // 2)
                        if 1 <= j <= HEADS:
                            attend_transpose(l, j - 1)
                        if j < HEADS - HG:
                            fill()
                    else:
                        if j >= 2:
                            attend_transpose(l, j - 2)
                        if j < HEADS:
                            attend_scores(l, j)
                        fill()
                        if j <= HEADS:
                            fill()
                        if j < HEADS - HG:
                            fill()
                        if odd:
                            attend_values(l, (j - 3) // 2)
                o_finish(l)

                transposes(2 * l + 1)
                f0 = l * LAYER_UNITS + ATT_UNITS
                up(l, 0, f0, 0, UP0, ln=2 * l + 1, wait_bank=False)
                up(l, 1, f0 + 1, 1, UP + 1, wait_bank=False)
                down(l, 0, f0 + 2, 2, 0, first=True)
                up(l, 2, f0 + 3, 3, UP)
                down(l, 1, f0 + 4, 0, 1)
                with pe.Fori(1, TRIPS) as i:
                    up(l, 2 * i + 1, f0 + 1 + 4 * i, 1, UP + 1)
                    down(l, 2 * i, f0 + 2 + 4 * i, 2, 0)
                    up(l, 2 * i + 2, f0 + 3 + 4 * i, 3, UP)
                    down(l, 2 * i + 1, f0 + 4 + 4 * i, 0, 1)
                up(l, CHUNKS - 1, f0 + 29, 1, UP + 1)
                last_units([(2, [uT(t, 0) for t in qkv], 0,
                             [(lo_done, f0 + 31), (uT_ready, CHUNKS * (l + 1) - 1)]),
                            (3, [uT(t, 1) for t in qkv], 0,
                             [(lo_done, f0 + 32), (uT_ready, CHUNKS * (l + 1))])])


INS = ["x", "rel_bias", "w_qkv", "w_o", "ln_mix_g", "ln_mix_b", "w_up", "w_down", "ln_ffn_g", "ln_ffn_b"]


def kernel(**inputs):
    import numpy as _np
    import concourse.bacc as _bacc
    from concourse import mybir as _mybir
    from concourse.bass_utils import run_bass_kernel_spmd as _run

    nc = _bacc.Bacc("TRN2", target_bir_lowering=False, num_devices=1)
    arrays, args = {}, []
    for name in INS:
        a = _np.ascontiguousarray(inputs[name])
        arrays[f"in_{name}_dram"] = a
        args.append(nc.dram_tensor(f"in_{name}_dram", a.shape, _mybir.dt.from_np(a.dtype), kind="ExternalInput").ap())
    args.append(nc.dram_tensor("out_0_dram", (1, SEQ, D), _mybir.dt.float32, kind="ExternalOutput").ap())
    build(nc, *args)
    r = _run(nc, [arrays], core_ids=[0])
    return r.results[0]["out_0_dram"]
```
